# Optimizing a Trainium2 kernel written in Bass

```python
import jax, jax.numpy as jnp
from jax import lax
import numpy as np

D_MODEL = 1024
BATCH = 1
SEQ = 4096
DEPTH = 1

N_MEM = 256
D_MIX = D_MODEL
D_GLA = D_MIX // 2
GLA_HEADS = 4
GLA_DK = (D_GLA // 2) // GLA_HEADS
GLA_DV = D_GLA // GLA_HEADS
GLA_RANK = 16
GLA_NORMALIZER = 16.0
CHUNK = 64
D_POOL = D_MIX // 4
POOL_WINDOWS = (2, 4, 8, 16)
POOL_GROUP = D_POOL // len(POOL_WINDOWS)
D_MEM = D_MIX - D_GLA - D_POOL
MEM_HEADS = 4
MEM_DH = D_MEM // MEM_HEADS
EPS = 1e-6

SPLIT_SIZES = (
    GLA_HEADS * GLA_DK,
    GLA_HEADS * GLA_DK,
    D_GLA,
    GLA_RANK,
    D_GLA,
    D_POOL,
    D_POOL,
    D_MEM,
    D_MEM,
)
D_IN = int(sum(SPLIT_SIZES))
SPLIT_IDX = [int(i) for i in np.cumsum(SPLIT_SIZES)[:-1]]

kernel_name = "hybrid_gla_pool_memxattn_block"

def rmsnorm(x, g):
    x32 = x.astype(jnp.float32)
    y = x32 * lax.rsqrt(jnp.mean(x32 * x32, axis=-1, keepdims=True) + EPS)
    return (y * g.astype(jnp.float32)).astype(x.dtype)

def gla_chunked(q, k, v, gk):
    B, T, H, dk = q.shape
    dv = v.shape[-1]
    n = T // CHUNK

    def to_chunks(a):
        return a.astype(jnp.float32).reshape(B, n, CHUNK, H, a.shape[-1]).transpose(0, 3, 1, 2, 4)

    q, k, v, gk = to_chunks(q) * (dk ** -0.5), to_chunks(k), to_chunks(v), to_chunks(gk)
    b = jnp.cumsum(gk, axis=3)
    q_d = q * jnp.exp(b)
    k_d = k * jnp.exp(-b)
    scores = jnp.einsum('bhnid,bhnjd->bhnij', q_d, k_d)
    tril = jnp.tril(jnp.ones((CHUNK, CHUNK), dtype=bool))
    scores = jnp.where(tril, scores, 0.0)
    o_intra = jnp.einsum('bhnij,bhnje->bhnie', scores, v)
    b_last = b[:, :, :, -1:, :]
    k_end = k * jnp.exp(b_last - b)
    chunk_state = jnp.einsum('bhncd,bhnce->bhnde', k_end, v)
    chunk_decay = jnp.exp(b_last[:, :, :, 0, :])

    def step(S, inp):
        dec, cs = inp
        return dec[..., None] * S + cs, S

    S0 = jnp.zeros((B, H, dk, dv), jnp.float32)
    _, S_prev = lax.scan(step, S0, (jnp.moveaxis(chunk_decay, 2, 0), jnp.moveaxis(chunk_state, 2, 0)))
    S_prev = jnp.moveaxis(S_prev, 0, 2)
    o_inter = jnp.einsum('bhncd,bhnde->bhnce', q_d, S_prev)
    o = o_intra + o_inter
    return o.transpose(0, 2, 3, 1, 4).reshape(B, T, H, dv)

def multiscale_pool(u):
    B, T, _ = u.shape
    u32 = u.astype(jnp.float32)
    cs = jnp.cumsum(u32, axis=1)
    W = max(POOL_WINDOWS)
    cs_pad = jnp.concatenate([jnp.zeros((B, W, D_POOL), jnp.float32), cs], axis=1)
    pos = jnp.arange(T)
    outs = []
    for g, w in enumerate(POOL_WINDOWS):
        lo, hi = g * POOL_GROUP, (g + 1) * POOL_GROUP
        c_now = cs[:, :, lo:hi]
        c_prev = cs_pad[:, W - w:W - w + T, lo:hi]
        count = jnp.minimum(pos + 1, w).astype(jnp.float32)[None, :, None]
        outs.append((c_now - c_prev) / count - u32[:, :, lo:hi])
    return jnp.stack(outs, axis=2)

def memory_attention(q_mem, mem_n, w_mem_kv):
    B, T, _ = q_mem.shape
    M = mem_n.shape[1]
    kv = mem_n @ w_mem_kv
    k_m, v_m = jnp.split(kv, 2, axis=-1)
    q = q_mem.reshape(B, T, MEM_HEADS, MEM_DH)
    k_m = k_m.reshape(B, M, MEM_HEADS, MEM_DH)
    v_m = v_m.reshape(B, M, MEM_HEADS, MEM_DH)
    s = jnp.einsum('bthd,bmhd->bhtm', q.astype(jnp.float32), k_m.astype(jnp.float32)) * (MEM_DH ** -0.5)
    p = jax.nn.softmax(s, axis=-1)
    o = jnp.einsum('bhtm,bmhd->bthd', p, v_m.astype(jnp.float32))
    return o.reshape(B, T, D_MEM)

def setup_inputs(seed: int = 0) -> dict:
    key = jax.random.key(seed)
    ks = jax.random.split(key, 14)
    f = jnp.float32
    return {
        "x": jax.random.normal(ks[0], (BATCH, SEQ, D_MODEL), f),
        "mem": jax.random.normal(ks[1], (BATCH, N_MEM, D_MODEL), f),
        "norm_g": 1.0 + 0.02 * jax.random.normal(ks[2], (D_MODEL,), f),
        "w_in": jax.random.normal(ks[3], (D_MODEL, D_IN), f) * D_MODEL ** -0.5,
        "w_gk_up": jax.random.normal(ks[4], (GLA_RANK, GLA_HEADS * GLA_DK), f) * GLA_RANK ** -0.5,
        "b_gk": 0.01 * jax.random.normal(ks[5], (GLA_HEADS * GLA_DK,), f),
        "gla_norm_g": 1.0 + 0.02 * jax.random.normal(ks[6], (GLA_DV,), f),
        "pool_w": jax.random.normal(ks[7], (len(POOL_WINDOWS), POOL_GROUP, POOL_GROUP), f) * POOL_GROUP ** -0.5,
        "pool_scale": 1.0 + 0.02 * jax.random.normal(ks[8], (D_POOL,), f),
        "mem_norm_g": 1.0 + 0.02 * jax.random.normal(ks[9], (D_MODEL,), f),
        "w_mem_kv": jax.random.normal(ks[10], (D_MODEL, 2 * D_MEM), f) * D_MODEL ** -0.5,
        "w_out": jax.random.normal(ks[11], (D_MIX, D_MODEL), f) * D_MIX ** -0.5,
        "final_g": 1.0 + 0.02 * jax.random.normal(ks[12], (D_MODEL,), f),
    }

def reference(x, mem, norm_g, w_in, w_gk_up, b_gk, gla_norm_g, pool_w, pool_scale,
              mem_norm_g, w_mem_kv, w_out, final_g):
    B, T, _ = x.shape
    dt = x.dtype
    mem_n = rmsnorm(mem, mem_norm_g)
    for _layer in range(DEPTH):
        h = rmsnorm(x, norm_g)
        proj = h @ w_in
        q_g, k_g, v_g, gk_lr, gate_g, u_p, gate_p, q_m, gate_m = jnp.split(proj, SPLIT_IDX, axis=-1)

        gk_logit = (gk_lr @ w_gk_up + b_gk).astype(jnp.float32)
        gk = jax.nn.log_sigmoid(gk_logit) / GLA_NORMALIZER
        o_gla = gla_chunked(q_g.reshape(B, T, GLA_HEADS, GLA_DK),
                            k_g.reshape(B, T, GLA_HEADS, GLA_DK),
                            v_g.reshape(B, T, GLA_HEADS, GLA_DV),
                            gk.reshape(B, T, GLA_HEADS, GLA_DK))
        o_gla = rmsnorm(o_gla, gla_norm_g).reshape(B, T, D_GLA)
        o_gla = (o_gla * jax.nn.silu(gate_g.astype(jnp.float32))).astype(dt)

        pooled = multiscale_pool(u_p)
        o_pool = jnp.einsum('btgp,gpq->btgq', pooled, pool_w.astype(jnp.float32)).reshape(B, T, D_POOL)
        o_pool = (o_pool * pool_scale.astype(jnp.float32) * jax.nn.silu(gate_p.astype(jnp.float32))).astype(dt)

        o_mem = memory_attention(q_m, mem_n, w_mem_kv)
        o_mem = (o_mem * jax.nn.silu(gate_m.astype(jnp.float32))).astype(dt)

        mixed = jnp.concatenate([o_gla, o_pool, o_mem], axis=-1)
        x = x + mixed @ w_out
    return rmsnorm(x, final_g)


_drawn_inputs = setup_inputs


def setup_inputs(seed=0):
    import zlib

    import numpy as np

    out = dict(_drawn_inputs(seed))
    spreads = {}
    factors = {'norm_g': 3.26,
     'b_gk': 52.401,
     'gla_norm_g': 194.51,
     'pool_scale': 110.64,
     'mem_norm_g': 63.144,
     'final_g': 24.219}
    for name, (base, spread) in spreads.items():
        noise = np.random.default_rng([zlib.crc32(name.encode()), seed]).standard_normal(out[name].shape)
        drawn = base * np.exp(spread * noise) if base else spread * noise
        out[name] = __import__('jax').numpy.asarray(drawn.astype(out[name].dtype))
    for name, factor in factors.items():
        out[name] = (out[name] * factor).astype(out[name].dtype)
    return out
```

```python
from contextlib import ExitStack

import numpy as np

import concourse.bass as bass
from concourse import mybir

ALU = mybir.AluOpType
ACT = mybir.ActivationFunctionType
AX = mybir.AxisListType
F32 = mybir.dt.float32
F16 = mybir.dt.float16
I32 = mybir.dt.int32
BF16 = mybir.dt.bfloat16
RMAX = bass.bass_isa.ReduceOp.absmax

P = 128
D = 1024
KT = D // P
TB = 256
NT = TB // P
CHUNK = 64
NC = TB // CHUNK
HEADS = 4
DK = 64
DV = 128
RANK = 16
NPAIR = HEADS // 2
NMEM = 256
MT = NMEM // P
HALO = 16
EPS = 1e-6
NORMALIZER = 16.0
QSCALE = DK ** -0.5
MSCALE = 64 ** -0.5

CQ, CK, CV, CG, CU, CGP, CGM, CQM, CLR = 0, 256, 512, 1024, 1536, 1792, 2048, 2304, 2560
DIN = CLR + RANK
WIDE = CLR

TOP = 14
EXP_MASK = 0x7F800000
SCALE_FIELD = float((127 + TOP + 127) << 23)
INV_FIELD = float(-(TOP << 23))
TINY = 2.0 ** -100
XBITS = 10

O_X, O_XN, O_MIX, O_T, O_U, O_QB = 0, 8192, 16384, 24576, 33024, 35200
O_KD, O_KE, O_V, O_WO, O_GATE = 39296, 41344, 43392, 47488, 80256
O_MHL, O_KAB, O_ST, O_S, O_Y, O_QM, O_END = 88448, 96640, 100736, 104832, 109952, 114048, 116096
O_TAIL = DIN * KT * 4


def hybrid_block(nc, xt, x, memt, w_in, w_ut, w_gk_up, vecs, pool_w, counts, w_mem, w_out, final_g, out):
    NB = xt.shape[0]
    ctx = ExitStack()
    with ctx:
        def sb(name, shape, dt):
            return ctx.enter_context(nc.sbuf_tensor(name, shape, dt))

        def sem(name):
            return ctx.enter_context(nc.semaphore(name))

        whl = sb("whl", [P, 2, KT, WIDE], F16)
        wlr = sb("wlr", [P, KT, 2 * RANK], F16)
        arena = sb("arena", [P, O_END // 4], F32)
        ident = sb("ident", [P, P], F32)
        ident16 = sb("ident16", [P, P], F16)
        ones = sb("ones", [P, P], F32)
        causal = sb("causal", [P, P], F32)
        keep = sb("keep", [P, TB], BF16)
        fg = sb("fg", [P, D], F32)
        kmt = sb("kmt", [P, NPAIR, 2, NMEM], F32)
        vm = sb("vm", [P, 2, MT, 256], F16)
        up2 = sb("up2", [2 * RANK, 256], F32)
        cnt = sb("cnt", [P, 2, HALO], F32)
        vec = sb("vec", [P, 32], F32)
        eps = sb("eps", [P, 2], F32)
        sca = sb("sca", [P, 24], F32)
        dec = sb("dec", [P, NPAIR, NC], F32)
        mx = sb("mx", [P, 8], F32)
        nm = sb("nm", [P, 8], F32)
        psum_p = sb("psum_p", [P, 8], F32)
        rsum = sb("rsum", [P, 8], F32)
        ysum = sb("ysum", [P, 2], F32)
        yr = sb("yr", [P, 2], F32)
        mmax = sb("mmax", [P, 4], F32)
        wmx = sb("wmx", [P, 2, KT], F32)
        idle = sb("idle", [P, 3], F32)

        g_in, g_mem, b_gk, g_out = vec[:, 0:8], vec[:, 8:16], vec[:, 16:18], vec[:, 18:26]

        def view(off, shape, dt):
            size = int(np.prod(shape)) * (2 if dt in (F16, BF16) else 4)
            ap = arena[:, off // 4:(off + size) // 4]
            if dt != F32:
                ap = ap.bitcast(dt)
            if len(shape) == 2:
                ap = ap.rearrange("p (a b) -> p a b", b=shape[1])
            if len(shape) == 3:
                ap = ap.rearrange("p (a b c) -> p a b c", b=shape[1], c=shape[2])
            if len(shape) == 4:
                ap = ap.rearrange("p (a b c d) -> p a b c d", b=shape[1], c=shape[2], d=shape[3])
            return ap

        xb = view(O_X, [KT, TB], F32)
        xn = view(O_XN, [2, KT, TB], F16)
        mixed = view(O_MIX, [KT, TB], F32)
        sq = view(O_MIX, [KT, TB], F32)
        ta = view(O_T, [2, TB], F32)
        tm = view(O_T + 2048, [2, TB], F32)
        tb = view(O_T + 4096, [2, TB], F32)
        te = view(O_T + 6144, [2, TB], F32)
        lrs = view(O_KE, [TB], F32)
        s2 = view(O_T, [2, HALO + TB], F32)
        s4 = view(O_T + 2176, [2, HALO + TB], F32)
        junk = view(O_T + 4352, [D], BF16)
        pr = [view(O_T + 2048 * b, [2, NMEM], F32) for b in range(2)]
        phl = [view(O_T + 4096 + 2048 * b, [2, 2, NMEM], F16) for b in range(2)]
        ub = view(O_U, [2, HALO + TB], F32)
        qb = view(O_QB, [NPAIR, 2, TB], F32)
        kd = view(O_KD, [NPAIR, TB], F32)
        ke = view(O_KE, [NPAIR, TB], F32)
        osq = view(O_KD, [2, TB], F32)
        orstd = view(O_KE, [2, TB], F32)
        v = view(O_V, [NT, 512], F32)
        wo = view(O_WO, [2, KT, D], F16)
        gate = view(O_GATE, [KT, TB], F32)
        mhl = view(O_MHL, [2, KT, TB], F16)
        pt = view(O_MHL, [NPAIR, 8, TB], F16)
        kab = view(O_KAB, [2, NT * NPAIR, P], F32)
        sT = view(O_ST, [NT, 2 * NPAIR, P], F32)
        S = view(O_S, [NC + 1, NPAIR, P], F32)
        yb = view(O_Y, [D], F32)
        qm = view(O_QM, [NPAIR, TB], F32)
        wraw = view(0, [KT, DIN], F32)
        woraw = view(O_TAIL, [KT, D], F32)
        memb = view(O_TAIL, [KT, NMEM], F32)
        wmraw = view(O_TAIL + 8192, [KT, 512], F32)
        wflat = whl[:, :, :, :].rearrange("p a b c -> p (a b c)").bitcast(F32)
        wut = wflat[:, 0:2048].rearrange("p (a b) -> p a b", a=2)
        pwb = wflat[:, 2048:2304].rearrange("p (a b) -> p a b", a=2)
        msq = wflat[:, 2304:2304 + KT * NMEM].rearrange("p (a b) -> p a b", a=KT)
        rmem = wflat[:, 4608:4608 + NMEM]
        vraw = wflat[:, 5120:5120 + 512].rearrange("p (a b) -> p a b", a=MT)

        bank = [ctx.enter_context(nc.psum_tensor(f"bank{i}", [P, 512], F32)) for i in range(8)]
        b16 = {i: bank[i][:, :].bitcast(F16) for i in (6, 7)}

        def col(n):
            return sca[:, n:n + 1]
        s_w, i_w, s_o, i_o, s_v, i_v, s_m, i_m, sc_in, sc_q, sc_out = (col(n) for n in range(11))
        gs = sca[:, 12:20]
        e_tmp = col(20)
        m_tmp = col(21)

        d_vec, d_mem, d_wut, d_wout, d_x, d_res, d_store = (
            sem(n) for n in ("d_vec", "d_mem", "d_wut", "d_wout", "d_x", "d_res", "d_store"))
        d_w = [sem(f"d_w{k}") for k in range(KT)]
        cleared, built, ident_ok, mem_sq, mem_sum, mem_ms, mem_ln, mem_r, mem_n = (
            sem(n) for n in ("cleared", "built", "ident_ok", "mem_sq", "mem_sum", "mem_ms", "mem_ln", "mem_r", "mem_n"))
        memk_done, memv_done, memk_out, memv_out, fold_done, fold_out = (
            sem(n) for n in ("memk_done", "memv_done", "memk_out", "memv_out", "fold_done", "fold_out"))
        max_in, max_all, prep, hi_w, lo_w, hi_v, hi_o, lo_o, scaled = (
            sem(n) for n in ("max_in", "max_all", "prep", "hi_w", "lo_w", "hi_v", "hi_o", "lo_o", "scaled"))
        pe_lr, pe_q, pe_k, pe_logit, pe_v, pe_p2, pe_out, pe_ket, pe_sc, pe_ms, pe_st, pe_rb, pe_pt, pe_o, pe_msq, pe_pv = (
            sem(n) for n in ("pe_lr", "pe_q", "pe_k", "pe_logit", "pe_v", "pe_p2", "pe_out", "pe_ket", "pe_sc",
                             "pe_ms", "pe_st", "pe_rb", "pe_pt", "pe_o", "pe_msq", "pe_pv"))
        lr_out, abs_ok, expabs, softplus, eb_ok, enb_ok, ebl_ok, v_out, p2_out, y_sq, y_ln, y_r, x_sq = (
            sem(n) for n in ("lr_out", "abs_ok", "expabs", "softplus", "eb_ok", "enb_ok", "ebl_ok", "v_out",
                             "p2_out", "y_sq", "y_ln", "y_r", "x_sq"))
        ket_out, p_exp, p_hi, rb_ln, rb_ok, x_hi, o_sq, o_ln, o_r, m_hi = (
            sem(n) for n in ("ket_out", "p_exp", "p_hi", "rb_ln", "rb_ok", "x_hi", "o_sq", "o_ln", "o_r", "m_hi"))
        z_ok, gk_ok, b_ok, bl_ok, q_ok, dec_ok, kd_ok, ke_ok, pooled, y_add, y_ok = (
            sem(n) for n in ("z_ok", "gk_ok", "b_ok", "bl_ok", "q_ok", "dec_ok", "kd_ok", "ke_ok", "pooled",
                             "y_add", "y_ok"))
        sT_ok, max_ok, nmax_ok, rs_ok, pn_ok, s_ok, pt_out, xn_ok, og_ok, mix_g, mix_m, mix_p, mmax_ok, m_sc, m_lo = (
            sem(n) for n in ("sT_ok", "max_ok", "nmax_ok", "rs_ok", "pn_ok", "s_ok", "pt_out", "xn_ok", "og_ok",
                             "mix_g", "mix_m", "mix_p", "mmax_ok", "m_sc", "m_lo"))
        w_sum, halo_ok, sq_add, p_lo, x_lo, m_all, s_carry = (
            sem(n) for n in ("w_sum", "halo_ok", "sq_add", "p_lo", "x_lo", "m_all", "s_carry"))

        block = ctx.enter_context(nc.Block())

        def run_blocks(eng, step, tail):
            step(0, True, False)
            with eng.Fori(1, NB - 1) as i:
                step(i, False, False)
            step(NB - 1, False, True)
            tail(NB)

        @block.sync
        def _(sp):
            sp.dma_start(vec[:, 0:26], vecs).then_inc(d_vec, 16)
            sp.dma_start(cnt[:, :, :], counts).then_inc(d_vec, 16)
            sp.dma_start(up2[0:RANK, :], w_gk_up).then_inc(d_vec, 16)
            sp.dma_start(up2[RANK:2 * RANK, :], w_gk_up).then_inc(d_vec, 16)
            sp.dma_start(fg[:, :], final_g.partition_broadcast(P)).then_inc(d_vec, 16)
            sp.dma_start(memb, memt).then_inc(d_mem, 16)
            sp.dma_start(wmraw, w_mem).then_inc(d_mem, 16)
            sp.dma_start(wut, w_ut).then_inc(d_wut, 16)
            sp.wait_ge(cleared, 1)
            for g in range(4):
                h = g % 2
                sp.dma_start(pwb[64 * h:64 * h + 64, g // 2, 64 * h:64 * h + 64], pool_w[g]).then_inc(d_wut, 16)
            for k in range(KT):
                sp.dma_start(wraw[:, k, 0:CU], w_in[:, k, 0:CU]).then_inc(d_w[k], 16)
                sp.dma_start(wraw[:, k, CGP:DIN], w_in[:, k, CU:DIN - 256]).then_inc(d_w[k], 16)
            sp.wait_ge(memk_done, 1)
            sp.wait_ge(memv_done, 1)
            sp.dma_start(woraw, w_out).then_inc(d_wout, 16)
            sp.wait_ge(hi_w, 1)
            sp.wait_ge(lo_w, 1)
            sp.dma_start(xb, xt[0]).then_inc(d_x, 16)

            def outputs(j, t):
                rows = bass.ds(j * TB + t * P, P)
                if isinstance(j, int) and j == 0 and t == 0:
                    sp.wait_ge(lo_o, KT)
                    sp.wait_ge(hi_o, KT)
                else:
                    sp.wait_ge(d_store, (j * NT + t) * 16)
                sp.dma_start(yb, x[rows, :]).then_inc(d_res, 16)
                sp.wait_ge(y_ok, j * NT + t + 1)
                sp.dma_start(out[rows, :], yb).then_inc(d_store, 16)

            def step(i, first, last):
                if not last:
                    sp.wait_ge(x_hi, i + 1)
                    sp.wait_ge(x_lo, i + 1)
                    sp.dma_start(xb, xt[i + 1] if first else xt[bass.ds(i + 1, 1)].rearrange(
                        "a p k t -> (a p) k t")).then_inc(d_x, 16)
                if not first:
                    for t in range(NT):
                        outputs(i - 1, t)

            def tail(n):
                for t in range(NT):
                    outputs(n - 1, t)
                sp.wait_ge(d_store, 16 * NT * n)

            run_blocks(sp, step, tail)

        @block.tensor
        def _(pe):
            pe.wait_ge(built, 3)
            pe.wait_ge(mem_sum, 3)
            nc.tensor.matmul(bank[0][:, 0:NMEM], ones[:, :], msq[:, 0, :], start=True, stop=True).then_inc(mem_ms, 1)
            pe.wait_ge(d_wut, 16 * 5)
            for k in range(KT):
                for g in range(2):
                    mm = nc.tensor.matmul(bank[4 + k // 2][:, (k % 2) * 256 + g * P:(k % 2) * 256 + g * P + P],
                                          wut[:, g, k * P:(k + 1) * P], pwb[:, g, :], start=True, stop=True)
            mm.then_inc(fold_done, 1)
            pe.wait_ge(mem_n, KT)
            for j in range(2):
                for k in range(KT):
                    mm = nc.tensor.matmul(bank[1][:, j * NMEM:(j + 1) * NMEM], wmraw[:, k, j * P:(j + 1) * P],
                                          memb[:, k, :], start=k == 0, stop=k == KT - 1)
            mm.then_inc(memk_done, 1)
            for j in range(MT):
                for k in range(KT):
                    mm = nc.tensor.matmul(bank[2][:, j * 256:(j + 1) * 256], memb[:, k, j * P:(j + 1) * P],
                                          wmraw[:, k, 256:512], start=k == 0, stop=k == KT - 1)
            mm.then_inc(memv_done, 1)

            def rms_sum(n):
                pe.wait_ge(sq_add, 3 * (n + 1))
                nc.tensor.matmul(bank[3][:, 0:TB], ones[:, :], sq[:, 0, :], start=True, stop=True).then_inc(pe_rb, 1)

            pe.wait_ge(memk_out, 2)
            rms_sum(0)

            def split(ap, tiles, parts):
                last = (tiles - 1, 2)
                for k in range(tiles):
                    for n, (a, b) in enumerate(((0, 0), (0, 1), (1, 0))):
                        lhs, rhs = parts(k, a, b)
                        mm = nc.tensor.matmul(ap, lhs, rhs, start=k == 0 and n == 0, stop=(k, n) == last)
                return mm

            def features(b, c0):
                for j in range(2):
                    c = c0 + j * P
                    mm = split(bank[b][:, j * TB:(j + 1) * TB], KT,
                               lambda k, p, r, c=c: (whl[:, p, k, c:c + P], xn[:, r, k, :]))
                return mm

            def out_proj(j, wait_bank):
                pe.wait_ge(m_hi, j + 1)
                pe.wait_ge(m_lo, j + 1)
                for t in range(NT):
                    for h in range(2):
                        wait_bank(2 * t + h)
                        split(bank[2 * t + h][:, :], KT,
                              lambda k, p, r: (mhl[:, p, k, t * P:(t + 1) * P],
                                               wo[:, r, k, h * 512:(h + 1) * 512])).then_inc(pe_out, 1)

            def step(i, first, last):
                if first:
                    pe.wait_ge(hi_w, KT + 1)
                    pe.wait_ge(lo_w, KT + 1)
                pe.wait_ge(x_hi, i + 1)
                pe.wait_ge(x_lo, i + 1)
                if not first:
                    pe.wait_ge(o_r, 2 * i)
                for r in range(2):
                    for k in range(KT):
                        mm = nc.tensor.matmul(bank[0][0:2 * RANK, 0:TB], wlr[:, k, :], xn[:, r, k, :],
                                              start=r == 0 and k == 0, stop=r == 1 and k == KT - 1)
                mm.then_inc(pe_lr, 1)
                features(1, CQ).then_inc(pe_q, 1)
                if not first:
                    pe.wait_ge(mix_m, i)
                features(2, CK).then_inc(pe_k, 1)
                pe.wait_ge(rb_ok, i + 1)
                pe.wait_ge(lr_out, i + 1)
                for j in range(2):
                    mm = nc.tensor.matmul(bank[3][:, j * TB:(j + 1) * TB], up2[:, j * P:(j + 1) * P],
                                          lrs[0:2 * RANK, :], start=True, stop=True)
                mm.then_inc(pe_logit, 1)
                for t in range(NT):
                    if t == 1:
                        pe.wait_ge(q_ok, 2 * (i + 1))
                    split(bank[t][:, :], KT, lambda k, p, r: (xn[:, p, k, t * P:(t + 1) * P],
                                                               whl[:, r, k, CV:CV + 512])).then_inc(pe_v, 1)
                pe.wait_ge(ke_ok, i + 1)
                features(2, CG).then_inc(pe_p2, 1)
                pe.wait_ge(z_ok, 2 * (i + 1))
                features(3, CG + 256).then_inc(pe_p2, 1)
                for n, c in enumerate((CU, CGP, CGM, CQM)):
                    if n < 2:
                        pe.wait_ge(v_out, 2 * i + n + 1)
                    else:
                        pe.wait_ge(p2_out, 6 * i + n - 1)
                    features(n, c).then_inc(pe_p2, 1)
                if not first:
                    out_proj(i - 1, lambda b: pe.wait_ge(p2_out, 6 * i + 3 + b))
                pe.wait_ge(ke_ok, i + 1)
                if not first:
                    pe.wait_ge(mix_g, 2 * i)
                else:
                    pe.wait_ge(fold_out, 4)
                for t in range(NT):
                    for p in range(NPAIR):
                        n = t * NPAIR + p
                        mm = nc.tensor.transpose(bank[4][:, n * P:(n + 1) * P], ke[:, p, t * P:(t + 1) * P],
                                                 ident[:, :])
                mm.then_inc(pe_ket, 1)
                pe.wait_ge(kd_ok, i + 1)
                pe.wait_ge(q_ok, 2 * (i + 1))
                for t in range(NT):
                    if not first:
                        pe.wait_ge(pt_out, 4 * i - 1 + t)
                    for p in range(NPAIR):
                        mm = nc.tensor.matmul(bank[6 + t][:, p * 256:(p + 1) * 256], kd[:, p, t * P:(t + 1) * P],
                                              qb[:, p, :, t * P:(t + 1) * P], start=True, stop=True)
                    mm.then_inc(pe_sc, 1)

                def mem_scores(n):
                    t, p = n // NPAIR, n % NPAIR
                    if first:
                        pe.wait_ge(p2_out, 6 * i + 3 + n)
                    else:
                        pe.wait_ge(y_add, 4 * (i - 1) + n + 1)
                    pe.wait_ge(p2_out, 6 * (i + 1))
                    nc.tensor.matmul(bank[n][:, :], qm[:, p, t * P:(t + 1) * P], kmt[:, p, :, :],
                                     start=True, stop=True).then_inc(pe_ms, 1)

                def state(c, b):
                    t, odd = c // 2, c % 2
                    for p in range(NPAIR):
                        mm = nc.tensor.matmul(bank[b][:, p * 256:(p + 1) * 256], kab[:, odd, t * NPAIR + p, :],
                                              v[:, t, p * 256:(p + 1) * 256], start=True, stop=True)
                    mm.then_inc(pe_st, 1)

                def turn_p(n, b):
                    pe.wait_ge(p_hi, 4 * i + n + 1)
                    pe.wait_ge(p_lo, 4 * i + n + 1)
                    for h in range(2):
                        for m in range(MT):
                            for r in range(2):
                                j = (h * MT + m) * 2 + r
                                mm = nc.tensor.transpose(b16[b][:, j * P:(j + 1) * P],
                                                         phl[n % 2][:, r, h, m * P:(m + 1) * P], ident16[:, :])
                    mm.then_inc(pe_pt, 1)

                def head_out(p, b):
                    for t in range(NT):
                        for h in range(2):
                            nc.tensor.matmul(bank[b][:, h * TB + t * P:h * TB + (t + 1) * P],
                                             v[:, t, (2 * p + h) * DV:(2 * p + h + 1) * DV],
                                             sT[:, t, 2 * p + h, :], start=t == 0 and h == 0, stop=False,
                                             skip_group_check=True)
                    o3 = bank[b][:, :].rearrange("p (h t) -> p h t", h=2)
                    for c in range(NC):
                        mm = nc.tensor.matmul(o3[:, :, c * CHUNK:(c + 1) * CHUNK], S[:, c, p, :],
                                              qb[:, p, :, c * CHUNK:(c + 1) * CHUNK], start=False,
                                              stop=c == NC - 1, skip_group_check=True)
                    mm.then_inc(pe_o, 1)

                def head_ms(p):
                    pe.wait_ge(p_exp, 4 * i + p + 1)
                    pe.wait_ge(o_sq, 2 * i + p + 1)
                    nc.tensor.matmul(bank[p][:, :], ones[:, :], osq, start=True, stop=True).then_inc(pe_msq, 1)

                mem_scores(0)
                mem_scores(1)
                pe.wait_ge(ket_out, 2 * (i + 1))
                pe.wait_ge(v_out, 2 * (i + 1))
                state(0, 5)
                mem_scores(2)
                mem_scores(3)
                state(1, 4)
                pe.wait_ge(sT_ok, 2 * i + 1)
                turn_p(0, 6)
                pe.wait_ge(s_ok, 4 * i + 1)
                state(2, 5)
                pe.wait_ge(sT_ok, 2 * i + 2)
                turn_p(1, 7)
                pe.wait_ge(s_ok, 4 * i + 2)
                state(3, 4)
                if not last:
                    pe.wait_ge(p_exp, 4 * i + 4)
                    rms_sum(i + 1)
                pe.wait_ge(pt_out, 4 * i + 1)
                turn_p(2, 6)
                pe.wait_ge(s_ok, 4 * i + 3)
                head_out(0, 5)
                pe.wait_ge(pt_out, 4 * i + 2)
                turn_p(3, 7)
                pe.wait_ge(s_ok, 4 * i + 4)
                head_out(1, 4)
                head_ms(0)
                pe.wait_ge(pt_out, 4 * i + 4)
                pe.wait_ge(p_exp, 4 * i + 3)
                for h in range(HEADS):
                    p, r0 = h // 2, 64 * (h % 2)
                    ps = bank[2][r0:r0 + 64, p * TB:(p + 1) * TB]
                    for m in range(MT):
                        for n, (a, b) in enumerate(((0, 0), (0, 1), (1, 0))):
                            mm = nc.tensor.matmul(ps, vm[:, a, m, h * 64:(h + 1) * 64],
                                                  pt[:, p, ((h % 2) * MT + m) * 2 + b, :],
                                                  start=m == 0 and n == 0, stop=m == MT - 1 and n == 2)
                mm.then_inc(pe_pv, 1)
                head_ms(1)

            def tail(n):
                def free(b):
                    if b < 2:
                        pe.wait_ge(o_r, 2 * n)
                    elif b == 2:
                        pe.wait_ge(mix_m, n)
                out_proj(n - 1, free)

            run_blocks(pe, step, tail)

        @block.scalar
        def _(act):
            act.wait_ge(d_mem, 32)
            nc.scalar.activation(msq, memb, ACT.Square).then_inc(mem_sq, 1)
            act.wait_ge(mem_ms, 1)
            act.wait_ge(built, 3)
            nc.scalar.activation(rmem, bank[0][:, 0:NMEM], ACT.Ln, bias=eps[:, 0:1], scale=1.0 / D).then_inc(mem_ln, 1)
            act.wait_ge(mem_ln, 1)
            nc.scalar.activation(rmem, rmem, ACT.Exp, scale=-0.5).then_inc(mem_r, 1)
            act.wait_ge(fold_done, 1)
            for n in range(4):
                nc.scalar.activation(wraw[:, 2 * n:2 * n + 2, CU:CU + 256],
                                     bank[4 + n][:, :].rearrange("p (a b) -> p a b", a=2), ACT.Copy).then_inc(fold_out, 1)
            act.wait_ge(memk_done, 1)
            act.wait_ge(cleared, 2)
            for h in range(2):
                r = slice(64 * h, 64 * h + 64)
                nc.scalar.activation(kmt[r, :, h, :], bank[1][r, :].rearrange("p (a b) -> p a b", a=2),
                                     ACT.Copy).then_inc(memk_out, 1)
            act.wait_ge(memv_done, 1)
            nc.scalar.activation(vraw, bank[2][:, :].rearrange("p (a b) -> p a b", a=MT), ACT.Copy).then_inc(memv_out, 1)
            act.wait_ge(scaled, 1)
            nc.scalar.activation(vm[:, 0, :, :], vraw, ACT.Copy, scale=s_v).then_inc(hi_v, 1)
            act.wait_ge(scaled, 2)
            act.wait_ge(prep, 1)
            for k in range(KT):
                nc.scalar.activation(whl[:, 0, k, :], wraw[:, k, 0:WIDE], ACT.Copy, scale=gs[:, k:k + 1]).then_inc(hi_w, 1)
            for k in range(KT):
                a = nc.scalar.activation(wlr[:, k, 0:RANK], wraw[:, k, CLR:DIN], ACT.Copy, scale=gs[:, k:k + 1])
            a.then_inc(hi_w, 1)

            def squares(n):
                act.wait_ge(d_x, 16 * (n + 1))
                nc.scalar.activation(sq, xb, ACT.Square).then_inc(x_sq, 1)

            def rstd(n):
                act.wait_ge(pe_rb, n + 1)
                nc.scalar.activation(sq[:, 1, :], bank[3][:, 0:TB], ACT.Ln, bias=eps[:, 0:1],
                                     scale=1.0 / D).then_inc(rb_ln, 1)
                act.wait_ge(rb_ln, n + 1)
                nc.scalar.activation(sq[:, 1, :], sq[:, 1, :], ACT.Exp, bias=eps[:, 1:2],
                                     scale=-0.5).then_inc(rb_ok, 1)

            def x_parts(n):
                act.wait_ge(xn_ok, n + 1)
                nc.scalar.activation(xn[:, 0, :, :], xb, ACT.Copy).then_inc(x_hi, 1)

            act.wait_ge(lo_w, KT + 1)
            squares(0)
            rstd(0)
            x_parts(0)
            act.wait_ge(scaled, 3)
            for k in range(KT):
                nc.scalar.activation(wo[:, 0, k, :], woraw[:, k, :], ACT.Copy, scale=g_out[:, k:k + 1]).then_inc(hi_o, 1)

            def mixed_hi(n):
                act.wait_ge(m_sc, n + 1)
                act.wait_ge(pe_pv, n + 1)
                nc.scalar.activation(mhl[:, 0, :, :], mixed, ACT.Copy, scale=s_m).then_inc(m_hi, 1)

            def norm_y(j):
                for t in range(NT):
                    act.wait_ge(y_add, 4 * j + 2 * t + 2)
                    nc.scalar.activation(junk, yb, ACT.Square, accum_out=ysum[:, 0:1]).then_inc(y_sq, 1)
                    act.wait_ge(y_sq, 2 * j + t + 1)
                    nc.scalar.activation(yr[:, 1:2], ysum[:, 0:1], ACT.Ln, bias=eps[:, 0:1],
                                         scale=1.0 / D).then_inc(y_ln, 1)
                    act.wait_ge(y_ln, 2 * j + t + 1)
                    nc.scalar.activation(yr[:, 0:1], yr[:, 1:2], ACT.Exp, scale=-0.5).then_inc(y_r, 1)

            def step(i, first, last):
                if not first:
                    mixed_hi(i - 1)
                act.wait_ge(pe_lr, i + 1)
                if not first:
                    act.wait_ge(mix_g, 2 * i)
                nc.scalar.activation(lrs[0:2 * RANK, :], bank[0][0:2 * RANK, 0:TB], ACT.Copy,
                                     scale=sc_in[0:2 * RANK, :]).then_inc(lr_out, 1)
                act.wait_ge(z_ok, 2 * (i + 1))
                nc.scalar.activation(ta, tm, ACT.Abs).then_inc(abs_ok, 1)
                act.wait_ge(abs_ok, i + 1)
                nc.scalar.activation(ta, ta, ACT.Exp, scale=-1.0).then_inc(expabs, 1)
                act.wait_ge(expabs, i + 1)
                nc.scalar.activation(ta, ta, ACT.Ln, bias=1.0).then_inc(softplus, 1)
                act.wait_ge(b_ok, 2 * (i + 1))
                nc.scalar.activation(te, tb, ACT.Exp, scale=1.0 / NORMALIZER).then_inc(eb_ok, 1)
                nc.scalar.activation(ta, tb, ACT.Exp, scale=-1.0 / NORMALIZER).then_inc(enb_ok, 1)
                act.wait_ge(bl_ok, i + 1)
                nc.scalar.activation(tm, tm, ACT.Exp, scale=1.0 / NORMALIZER).then_inc(ebl_ok, 1)
                for t in range(NT):
                    act.wait_ge(pe_v, 2 * i + t + 1)
                    nc.scalar.activation(v[:, t, :], bank[t][:, :], ACT.Copy, scale=sc_in).then_inc(v_out, 1)
                if first:
                    act.wait_ge(lo_o, KT)
                    act.wait_ge(hi_o, KT)

                def silu(n, b, g):
                    act.wait_ge(pe_p2, 6 * i + n)
                    nc.scalar.activation(gate[:, g:g + 2, :], bank[b][:, :].rearrange("p (a t) -> p a t", a=2),
                                         ACT.Silu, scale=sc_in).then_inc(p2_out, 1)

                silu(1, 2, 0)
                silu(2, 3, 2)
                act.wait_ge(pe_p2, 6 * i + 3)
                act.wait_ge(halo_ok, i + 1)
                nc.scalar.activation(ub[:, :, HALO:], bank[0][:, :].rearrange("p (a t) -> p a t", a=2), ACT.Copy,
                                     scale=sc_in).then_inc(p2_out, 1)
                silu(4, 1, 4)
                silu(5, 2, 6)
                act.wait_ge(pe_p2, 6 * i + 6)
                nc.scalar.activation(qm, bank[3][:, :].rearrange("p (a t) -> p a t", a=2), ACT.Copy,
                                     scale=sc_in).then_inc(p2_out, 1)
                if not last:
                    if not first:
                        act.wait_ge(m_lo, i)
                    squares(i + 1)
                if not first:
                    act.wait_ge(pooled, 4 * (i + 1))
                    norm_y(i - 1)
                act.wait_ge(pe_ket, i + 1)
                if first:
                    act.wait_ge(cleared, 4)
                for odd in range(2):
                    r = slice(64 * odd, 64 * odd + 64)
                    nc.scalar.activation(kab[r, odd, :, :], bank[4][r, :].rearrange("p (a b) -> p a b", b=P),
                                         ACT.Copy).then_inc(ket_out, 1)

                def p_exp_of(n):
                    act.wait_ge(nmax_ok, 4 * i + n + 1)
                    if n >= 2:
                        act.wait_ge(p_lo, 4 * i + n - 1)
                    else:
                        act.wait_ge(pooled, 4 * (i + 1))
                        if not first:
                            act.wait_ge(pe_pt, 4 * i)
                    for h in range(2):
                        a = nc.scalar.activation(pr[n % 2][:, h, :], bank[n][:, h * 256:(h + 1) * 256], ACT.Exp,
                                                 bias=nm[:, 2 * n + h:2 * n + h + 1], scale=MSCALE,
                                                 accum_out=psum_p[:, 2 * n + h:2 * n + h + 1])
                    a.then_inc(p_exp, 1)

                def p_hi_of(n):
                    act.wait_ge(pn_ok, 4 * i + n + 1)
                    if n >= 2:
                        act.wait_ge(pe_pt, 4 * i + n - 1)
                    nc.scalar.activation(phl[n % 2][:, 0, :, :], pr[n % 2], ACT.Copy).then_inc(p_hi, 1)

                p_exp_of(0)
                p_exp_of(1)
                p_hi_of(0)
                p_hi_of(1)
                p_exp_of(2)
                p_exp_of(3)
                if not last:
                    rstd(i + 1)
                p_hi_of(2)
                p_hi_of(3)

                def o_square(p, b):
                    act.wait_ge(pe_o, 2 * i + p + 1)
                    if p:
                        act.wait_ge(pe_msq, 2 * i + 1)
                    nc.scalar.activation(osq, bank[b][:, :].rearrange("p (a t) -> p a t", a=2),
                                         ACT.Square).then_inc(o_sq, 1)

                def o_rstd(p):
                    act.wait_ge(pe_msq, 2 * i + p + 1)
                    if p:
                        act.wait_ge(mix_g, 2 * i + 1)
                    nc.scalar.activation(orstd, bank[p][:, :].rearrange("p (a t) -> p a t", a=2), ACT.Ln,
                                         bias=eps[:, 0:1], scale=1.0 / DV).then_inc(o_ln, 1)
                    act.wait_ge(o_ln, 2 * i + p + 1)
                    nc.scalar.activation(orstd, orstd, ACT.Exp, scale=-0.5).then_inc(o_r, 1)

                o_square(0, 5)
                if not last:
                    x_parts(i + 1)
                o_rstd(0)
                o_square(1, 4)
                o_rstd(1)

            def tail(n):
                mixed_hi(n - 1)
                norm_y(n - 1)

            run_blocks(act, step, tail)

        @block.vector
        def _(dve):
            nc.vector.memset(pwb, 0.0).then_inc(cleared, 1)
            nc.vector.memset(kmt[:, :, :, :], 0.0).then_inc(cleared, 1)
            nc.vector.memset(keep[:, :], 1.0).then_inc(gk_ok, 1)
            dve.wait_ge(gk_ok, 1)
            nc.vector.memset(keep[:, 0:TB:CHUNK], 0.0).then_inc(gk_ok, 1)
            dve.wait_ge(d_vec, 16 * 5)
            dve.wait_ge(mem_r, 1)
            for k in range(KT):
                nc.vector.scalar_tensor_tensor(memb[:, k, :], memb[:, k, :], g_mem[:, k:k + 1], rmem,
                                               ALU.mult, ALU.mult).then_inc(mem_n, 1)

            steps = [0]

            def after(ins):
                steps[0] += 1
                ins.then_inc(max_in, 1)
                dve.wait_ge(max_in, steps[0])

            def exponents(src, s, inv):
                after(nc.vector.tensor_scalar(m_tmp, src, TINY, None, ALU.max))
                after(nc.vector.tensor_scalar(e_tmp.bitcast(I32), m_tmp.bitcast(I32), EXP_MASK, None, ALU.bitwise_and))
                nc.vector.tensor_scalar(s.bitcast(I32), e_tmp.bitcast(I32), -1.0, SCALE_FIELD, ALU.mult, ALU.add)
                after(nc.vector.tensor_scalar(inv.bitcast(I32), e_tmp.bitcast(I32), INV_FIELD, None, ALU.add))

            dve.wait_ge(memv_out, 1)
            after(nc.vector.tensor_reduce(mmax[:, 0:1], vraw, AX.XY, ALU.max, apply_absolute_value=True))
            nc.vector.tensor_copy(mmax[:, 1:2], mmax[:, 0:1]).then_inc(mmax_ok, 1)
            dve.wait_ge(max_all, 1)
            exponents(mmax[:, 2:3], s_v, i_v)
            nc.vector.tensor_copy(mmax[:, 3:4], mmax[:, 2:3]).then_inc(scaled, 1)
            dve.wait_ge(hi_v, 1)
            nc.vector.scalar_tensor_tensor(vm[:, 1, :, :], vraw, s_v, vm[:, 0, :, :], ALU.mult,
                                           ALU.subtract).then_inc(prep, 1)
            dve.wait_ge(fold_out, 4)
            for k in range(KT):
                dve.wait_ge(d_w[k], 32)
                a = nc.vector.tensor_reduce(wmx[:, 0, k:k + 1], wraw[:, k, :], AX.X, ALU.max, apply_absolute_value=True)
            after(a)
            after(nc.vector.tensor_tensor(wmx[:, 0, :], wmx[:, 0, :], g_in, ALU.mult))
            nc.vector.tensor_reduce(mmax[:, 1:2], wmx[:, 0, :], AX.X, ALU.max,
                                    apply_absolute_value=True).then_inc(mmax_ok, 1)
            dve.wait_ge(max_all, 2)
            exponents(mmax[:, 2:3], s_w, i_w)
            after(nc.vector.tensor_scalar(gs, g_in, s_w, None, ALU.mult))
            nc.vector.tensor_scalar(sc_q, i_w, 2.0 ** -XBITS * QSCALE, None, ALU.mult)
            nc.vector.tensor_scalar(sc_in, i_w, 2.0 ** -XBITS, None, ALU.mult).then_inc(scaled, 1)
            for k in range(KT):
                dve.wait_ge(hi_w, k + 1)
                nc.vector.scalar_tensor_tensor(whl[:, 1, k, :], wraw[:, k, 0:WIDE], gs[:, k:k + 1], whl[:, 0, k, :],
                                               ALU.mult, ALU.subtract).then_inc(lo_w, 1)
            dve.wait_ge(hi_w, KT + 1)
            for k in range(KT):
                a = nc.vector.scalar_tensor_tensor(wlr[:, k, RANK:], wraw[:, k, CLR:DIN], gs[:, k:k + 1],
                                                   wlr[:, k, 0:RANK], ALU.mult, ALU.subtract)
            a.then_inc(lo_w, 1)

            def normalise(n):
                dve.wait_ge(rb_ok, n + 1)
                r = sq[:, 1:2, :].broadcast_to([P, KT, TB])
                nc.vector.tensor_tensor(xb, xb, r, ALU.mult).then_inc(xn_ok, 1)

            normalise(0)
            dve.wait_ge(d_wout, 16)
            for k in range(KT):
                a = nc.vector.tensor_reduce(wmx[:, 1, k:k + 1], woraw[:, k, :], AX.X, ALU.max, apply_absolute_value=True)
            after(a)
            after(nc.vector.tensor_tensor(wmx[:, 1, :], wmx[:, 1, :], g_out, ALU.mult))
            nc.vector.tensor_reduce(mmax[:, 1:2], wmx[:, 1, :], AX.X, ALU.max,
                                    apply_absolute_value=True).then_inc(mmax_ok, 1)
            dve.wait_ge(max_all, 3)
            exponents(mmax[:, 2:3], s_o, i_o)
            after(nc.vector.tensor_scalar(g_out, g_out, s_o, None, ALU.mult))
            nc.vector.tensor_copy(mmax[:, 3:4], mmax[:, 2:3]).then_inc(scaled, 1)
            for k in range(KT):
                dve.wait_ge(hi_o, k + 1)
                nc.vector.scalar_tensor_tensor(wo[:, 1, k, :], woraw[:, k, :], g_out[:, k:k + 1], wo[:, 0, k, :],
                                               ALU.mult, ALU.subtract).then_inc(lo_o, 1)

            def mixed_lo(n):
                dve.wait_ge(m_all, n + 1)
                nc.vector.tensor_scalar(m_tmp, mmax[:, 2:3], TINY, None, ALU.max).then_inc(m_tiny, 1)
                dve.wait_ge(m_tiny, n + 1)
                nc.vector.tensor_scalar(e_tmp.bitcast(I32), m_tmp.bitcast(I32), EXP_MASK, None,
                                        ALU.bitwise_and).then_inc(m_exp, 1)
                dve.wait_ge(m_exp, n + 1)
                nc.vector.tensor_scalar(i_m.bitcast(I32), e_tmp.bitcast(I32), INV_FIELD, None,
                                        ALU.add).then_inc(m_inv, 1)
                nc.vector.tensor_scalar(s_m.bitcast(I32), e_tmp.bitcast(I32), -1.0, SCALE_FIELD, ALU.mult,
                                        ALU.add).then_inc(m_sc, 1)
                dve.wait_ge(m_inv, n + 1)
                nc.vector.tensor_scalar(sc_out, i_m, i_o, None, ALU.mult).then_inc(sc_ok, 1)
                dve.wait_ge(m_hi, n + 1)
                nc.vector.scalar_tensor_tensor(mhl[:, 1, :, :], mixed, s_m, mhl[:, 0, :, :], ALU.mult,
                                               ALU.subtract).then_inc(m_lo, 1)

            def outputs(j):
                dve.wait_ge(sc_ok, j + 1)
                for t in range(NT):
                    dve.wait_ge(d_res, 16 * (NT * j + t + 1))
                    for h in range(2):
                        dve.wait_ge(pe_out, 4 * j + 2 * t + h + 1)
                        c = slice(h * 512, (h + 1) * 512)
                        nc.vector.scalar_tensor_tensor(yb[:, c], bank[2 * t + h][:, :], sc_out, yb[:, c], ALU.mult,
                                                       ALU.add).then_inc(y_add, 1)
                    dve.wait_ge(y_add, 4 * j + 2 * t + 2)
                    dve.wait_ge(y_r, NT * j + t + 1)
                    nc.vector.scalar_tensor_tensor(yb, yb, yr[:, 0:1], fg[:, :], ALU.mult,
                                                   ALU.mult).then_inc(y_ok, 1)

            def step(i, first, last):
                if not first:
                    mixed_lo(i - 1)
                dve.wait_ge(pe_logit, i + 1)
                if not first:
                    dve.wait_ge(p_lo, 4 * i)
                    dve.wait_ge(pe_pt, 4 * i)
                for j in range(2):
                    nc.vector.tensor_scalar(tm[:, j, :], bank[3][:, j * TB:(j + 1) * TB], b_gk[:, j:j + 1], None,
                                            ALU.add).then_inc(z_ok, 1)
                dve.wait_ge(z_ok, 2 * (i + 1))
                dve.wait_ge(softplus, i + 1)
                nc.vector.scalar_tensor_tensor(tm, tm, 0.0, ta, ALU.min, ALU.subtract).then_inc(gk_ok, 1)
                dve.wait_ge(gk_ok, i + 3)
                for j in range(2):
                    nc.vector.tensor_tensor_scan(tb[:, j, :], keep[:, :], tm[:, j, :], 0.0, ALU.mult,
                                                 ALU.add).then_inc(b_ok, 1)
                dve.wait_ge(b_ok, 2 * (i + 1))
                b4 = tb.rearrange("p a (c t) -> p (a c) t", t=CHUNK)
                nc.vector.tensor_tensor(tm.rearrange("p a (c t) -> p (a c) t", t=CHUNK),
                                        b4[:, :, CHUNK - 1:CHUNK].broadcast_to([P, 2 * NC, CHUNK]), b4,
                                        ALU.subtract).then_inc(bl_ok, 1)
                dve.wait_ge(eb_ok, i + 1)
                dve.wait_ge(pe_q, i + 1)
                if first:
                    dve.wait_ge(cleared, 5)
                else:
                    dve.wait_ge(pe_o, 2 * i)
                for h in range(2):
                    r = slice(64 * h, 64 * h + 64)
                    nc.vector.scalar_tensor_tensor(qb[r, :, h, :], bank[1][r, :].rearrange("p (a t) -> p a t", a=2),
                                                   sc_q[r, :], te[r, :, :], ALU.mult, ALU.mult).then_inc(q_ok, 1)
                nc.vector.tensor_copy(dec[:, :, :], te[:, :, CHUNK - 1:TB:CHUNK]).then_inc(dec_ok, 1)
                dve.wait_ge(enb_ok, i + 1)
                dve.wait_ge(pe_k, i + 1)
                if not first:
                    dve.wait_ge(pe_msq, 2 * i)
                k3 = bank[2][:, :].rearrange("p (a t) -> p a t", a=2)
                nc.vector.scalar_tensor_tensor(kd, k3, sc_in, ta, ALU.mult, ALU.mult).then_inc(kd_ok, 1)
                dve.wait_ge(ebl_ok, i + 1)
                nc.vector.scalar_tensor_tensor(ke, k3, sc_in, tm, ALU.mult, ALU.mult).then_inc(ke_ok, 1)
                for w, (r, a, s) in enumerate(((0, 0, s2), (64, 0, s4), (0, 1, s2), (64, 1, s4))):
                    dve.wait_ge(w_sum, 4 * (i + 1))
                    dve.wait_ge(halo_ok, i + 2)
                    rr = slice(r, r + 64)
                    inv = 1.0 / (2, 4, 8, 16)[w]
                    if not first:
                        nc.vector.scalar_tensor_tensor(ub[rr, a, HALO:], s[rr, a, HALO:], inv, ub[rr, a, HALO:],
                                                       ALU.mult, ALU.subtract).then_inc(pooled, 1)
                    else:
                        nc.vector.tensor_tensor(s[rr, a, HALO:2 * HALO], s[rr, a, HALO:2 * HALO], cnt[rr, a, :],
                                                ALU.mult).then_inc(cut, 1)
                        nc.vector.scalar_tensor_tensor(ub[rr, a, 2 * HALO:], s[rr, a, 2 * HALO:], inv,
                                                       ub[rr, a, 2 * HALO:], ALU.mult, ALU.subtract)
                        dve.wait_ge(cut, w + 1)
                        nc.vector.tensor_tensor(ub[rr, a, HALO:2 * HALO], s[rr, a, HALO:2 * HALO],
                                                ub[rr, a, HALO:2 * HALO], ALU.subtract).then_inc(pooled, 1)
                if not first:
                    outputs(i - 1)
                mask = causal[:, :].bitcast(I32).unsqueeze(1).broadcast_to([P, 4, P])

                def masked(t):
                    if first:
                        dve.wait_ge(built, 3)
                        dve.wait_ge(cleared, 5)
                    dve.wait_ge(pe_sc, 2 * i + t + 1)
                    nc.vector.memset(idle[:, t:t + 1], 0.0)
                    nc.vector.copy_predicated(sT[:, t, :, :], mask, bank[6 + t][:, :].rearrange("p (a b) -> p a b", b=P)
                                              ).then_inc(sT_ok, 1)

                def mem_max(n):
                    dve.wait_ge(pe_ms, 4 * i + n + 1)
                    nc.vector.tensor_reduce(mx[:, 2 * n:2 * n + 2], bank[n][:, :].rearrange("p (h m) -> p h m", h=2),
                                            AX.X, ALU.max).then_inc(max_ok, 1)
                    dve.wait_ge(max_ok, 4 * i + n + 1)
                    nc.vector.tensor_scalar(nm[:, 2 * n:2 * n + 2], mx[:, 2 * n:2 * n + 2], -MSCALE, None,
                                            ALU.mult).then_inc(nmax_ok, 1)

                def p_norm(n):
                    dve.wait_ge(p_exp, 4 * i + n + 1)
                    nc.vector.reciprocal(rsum[:, 2 * n:2 * n + 2], psum_p[:, 2 * n:2 * n + 2]).then_inc(rs_ok, 1)
                    dve.wait_ge(rs_ok, 4 * i + n + 1)
                    r = rsum[:, 2 * n:2 * n + 2].unsqueeze(2).broadcast_to([P, 2, NMEM])
                    nc.vector.tensor_tensor(pr[n % 2], pr[n % 2], r, ALU.mult).then_inc(pn_ok, 1)

                def state(c, b):
                    dve.wait_ge(pe_st, 4 * i + c + 1)
                    if c == 0:
                        dve.wait_ge(s_carry, i + 1)
                        dve.wait_ge(dec_ok, i + 1)
                    else:
                        dve.wait_ge(s_ok, 4 * i + c)
                    for p in range(NPAIR):
                        for h in range(2):
                            r = slice(64 * h, 64 * h + 64)
                            a = nc.vector.scalar_tensor_tensor(
                                S[r, c + 1, p, :], S[r, c, p, :], dec[r, p, c:c + 1],
                                bank[b][r, p * 256 + h * P:p * 256 + (h + 1) * P], ALU.mult, ALU.add)
                    a.then_inc(s_ok, 1)

                def pt_copy(n, b):
                    t, p = n // NPAIR, n % NPAIR
                    dve.wait_ge(pe_pt, 4 * i + n + 1)
                    if not first:
                        dve.wait_ge(pe_out, 4 * i)
                    nc.vector.tensor_copy(pt[:, p, :, t * P:(t + 1) * P],
                                          b16[b].rearrange("p (a b) -> p a b", b=P)).then_inc(pt_out, 1)

                def head(p, b):
                    dve.wait_ge(o_r, 2 * i + p + 1)
                    nc.vector.tensor_tensor(orstd, orstd, gate[:, 2 * p:2 * p + 2, :], ALU.mult).then_inc(og_ok, 1)
                    dve.wait_ge(og_ok, 2 * i + p + 1)
                    nc.vector.tensor_tensor(mixed[:, 2 * p:2 * p + 2, :], bank[b][:, :].rearrange("p (a t) -> p a t", a=2),
                                            orstd, ALU.mult).then_inc(mix_g, 1)

                masked(0)
                masked(1)
                mem_max(0)
                mem_max(1)
                p_norm(0)
                state(0, 5)
                p_norm(1)
                mem_max(2)
                mem_max(3)
                state(1, 4)
                pt_copy(0, 6)
                state(2, 5)
                p_norm(2)
                pt_copy(1, 7)
                state(3, 4)
                p_norm(3)
                if not last:
                    normalise(i + 1)
                if not last:
                    dve.wait_ge(xn_ok, i + 2)
                dve.wait_ge(p2_out, 6 * i + 5)
                dve.wait_ge(pooled, 4 * (i + 1))
                nc.vector.tensor_tensor(mixed[:, 4:6, :], ub[:, :, HALO:], gate[:, 4:6, :], ALU.mult).then_inc(mix_p, 1)
                pt_copy(2, 6)
                pt_copy(3, 7)
                head(0, 5)
                dve.wait_ge(pe_pv, i + 1)
                nc.vector.scalar_tensor_tensor(mixed[:, 6:8, :], bank[2][:, :].rearrange("p (a t) -> p a t", a=2), i_v,
                                               gate[:, 6:8, :], ALU.mult, ALU.mult).then_inc(mix_m, 1)
                head(1, 4)
                dve.wait_ge(mix_p, i + 1)
                dve.wait_ge(mix_m, i + 1)
                dve.wait_ge(mix_g, 2 * (i + 1))
                nc.vector.tensor_reduce(mmax[:, 1:2], mixed, AX.XY, ALU.max,
                                        apply_absolute_value=True).then_inc(mmax_ok, 1)

            def tail(n):
                mixed_lo(n - 1)
                outputs(n - 1)

            m_tiny, m_exp, m_inv, sc_ok, cut = (sem(n) for n in ("m_tiny", "m_exp", "m_inv", "sc_ok", "cut"))
            run_blocks(dve, step, tail)

        @block.gpsimd
        def _(pool):
            nc.gpsimd.memset(ones[:, :], 1.0).then_inc(built, 1)
            nc.gpsimd.memset(eps[:, 0:1], EPS)
            nc.gpsimd.memset(eps[:, 1:2], float(np.log(2.0 ** XBITS)))
            nc.gpsimd.memset(ident[:, :], 0.0).then_inc(ident_ok, 1)
            nc.gpsimd.memset(causal[:, :], 1.0).then_inc(ident_ok, 1)
            pool.wait_ge(ident_ok, 2)
            nc.gpsimd.affine_select(out=ident[:, :], in_=ident[:, :], compare_op=ALU.not_equal, fill=1.0, base=0,
                                    pattern=[[-1, P]], channel_multiplier=1).then_inc(ident_ok, 1)
            nc.gpsimd.affine_select(out=causal[:, :], in_=causal[:, :], compare_op=ALU.is_ge, fill=0.0, base=0,
                                    pattern=[[1, P]], channel_multiplier=-1).then_inc(ident_ok, 1)
            pool.wait_ge(ident_ok, 4)
            nc.gpsimd.memset(causal[0:64, 64:128], 0.0).then_inc(built, 1)
            nc.gpsimd.tensor_copy(ident16[:, :], ident[:, :]).then_inc(built, 1)

            def fold_rows(buf, n0, signal):
                for n, half in enumerate((4, 2, 1)):
                    if n:
                        pool.wait_ge(signal, n0 + n)
                    nc.gpsimd.tensor_tensor(buf[:, 0:half, :], buf[:, 0:half, :], buf[:, half:2 * half, :],
                                            ALU.add).then_inc(signal, 1)

            pool.wait_ge(mem_sq, 1)
            fold_rows(msq, 0, mem_sum)
            for n in range(3):
                pool.wait_ge(mmax_ok, n + 1)
                nc.gpsimd.partition_all_reduce(mmax[:, 2:3], mmax[:, 1:2], P, RMAX).then_inc(max_all, 1)
                if n == 1:
                    pool.wait_ge(x_sq, 1)
                    fold_rows(sq, 0, sq_add)
                    pool.wait_ge(x_hi, 1)
                    nc.gpsimd.tensor_tensor(xn[:, 1, :, :], xb, xn[:, 0, :, :], ALU.subtract).then_inc(x_lo, 1)
            pool.wait_ge(lo_w, KT + 1)
            nc.gpsimd.memset(ub[:, :, 0:HALO], 0.0).then_inc(halo_ok, 1)
            nc.gpsimd.memset(qb, 0.0).then_inc(cleared, 1)
            pool.wait_ge(hi_o, KT)
            pool.wait_ge(lo_o, KT)
            nc.gpsimd.memset(kab, 0.0).then_inc(cleared, 1)
            nc.gpsimd.memset(sT, 0.0).then_inc(cleared, 1)
            nc.gpsimd.memset(S[:, 0, :, :], 0.0).then_inc(s_carry, 1)

            def x_lo_of(n):
                pool.wait_ge(x_hi, n + 1)
                nc.gpsimd.tensor_tensor(xn[:, 1, :, :], xb, xn[:, 0, :, :], ALU.subtract).then_inc(x_lo, 1)

            def p_lo_of(i, n):
                pool.wait_ge(p_hi, 4 * i + n + 1)
                nc.gpsimd.tensor_tensor(phl[n % 2][:, 1, :, :], pr[n % 2], phl[n % 2][:, 0, :, :],
                                        ALU.subtract).then_inc(p_lo, 1)

            def step(i, first, last):
                L = HALO + TB
                pool.wait_ge(p2_out, 6 * i + 3)
                pool.wait_ge(ke_ok, i + 1)
                pool.wait_ge(q_ok, 2 * (i + 1))
                nc.gpsimd.tensor_tensor(s2[:, :, 1:L], ub[:, :, 1:L], ub[:, :, 0:L - 1], ALU.add).then_inc(w_sum, 1)
                pool.wait_ge(w_sum, 4 * i + 1)
                nc.gpsimd.tensor_tensor(s4[:, :, 3:L], s2[:, :, 3:L], s2[:, :, 1:L - 2], ALU.add).then_inc(w_sum, 1)
                nc.gpsimd.tensor_copy(ub[:, :, 0:HALO], ub[:, :, TB:TB + HALO]).then_inc(halo_ok, 1)
                pool.wait_ge(w_sum, 4 * i + 2)
                nc.gpsimd.tensor_tensor(s2[:, 1, 7:L], s4[:, 1, 7:L], s4[:, 1, 3:L - 4], ALU.add).then_inc(w_sum, 1)
                pool.wait_ge(w_sum, 4 * i + 3)
                nc.gpsimd.tensor_tensor(s4[:, 1, 15:L], s2[:, 1, 15:L], s2[:, 1, 7:L - 8], ALU.add).then_inc(w_sum, 1)
                if not last:
                    pool.wait_ge(x_sq, i + 2)
                    fold_rows(sq, 3 * (i + 1), sq_add)
                for n in range(4):
                    p_lo_of(i, n)
                if not last:
                    x_lo_of(i + 1)
                if not first:
                    pool.wait_ge(m_sc, i)
                pool.wait_ge(mmax_ok, i + 4)
                nc.gpsimd.tensor_tensor(idle[:, 2:3], eps[:, 0:1], eps[:, 1:2], ALU.add)
                nc.gpsimd.tensor_copy(S[:, 0, :, :], S[:, NC, :, :]).then_inc(s_carry, 1)
                nc.gpsimd.partition_all_reduce(mmax[:, 2:3], mmax[:, 1:2], P, RMAX).then_inc(m_all, 1)

            run_blocks(pool, step, lambda n: None)


def kernel(**inputs):
    import concourse.bacc as bacc
    from concourse.bass_utils import run_bass_kernel_spmd

    a = {k: np.asarray(v) for k, v in inputs.items()}
    T = a["x"].shape[1]

    def tiled(w):
        return np.ascontiguousarray(w.reshape(-1, P, w.shape[1]).transpose(1, 0, 2))

    def column(g):
        return g.reshape(-1, P).T

    w = a["w_in"]
    sizes = (256, 256, 512, RANK, 512, 256, 256, 256, 256)
    q, k, v, lr, gg, u, gp, qm, gm = np.split(w, np.cumsum(sizes)[:-1], axis=1)
    counts = np.zeros((P, 2, HALO), np.float32)
    for g, win in enumerate((2, 4, 8, 16)):
        counts[64 * (g % 2):64 * (g % 2) + 64, g // 2] = 1.0 / np.minimum(np.arange(HALO) + 1, win)
    unit = np.ones((P, 2), np.float32)
    arrays = {
        "xt": np.ascontiguousarray(a["x"][0].T.reshape(KT, P, T // TB, TB).transpose(2, 1, 0, 3)),
        "x": np.ascontiguousarray(a["x"][0]),
        "memt": tiled(np.ascontiguousarray(a["mem"][0].T)),
        "w_in": tiled(np.concatenate([q, k, v, gg, gp, gm, qm, lr], axis=1)),
        "w_ut": tiled(np.ascontiguousarray(u.T)),
        "w_gk_up": np.ascontiguousarray(a["w_gk_up"]),
        "vecs": np.ascontiguousarray(np.concatenate(
            [column(a["norm_g"]), column(a["mem_norm_g"]), column(a["b_gk"])]
            + [column(a["gla_norm_g"])] * HEADS + [column(a["pool_scale"]), unit], axis=1)),
        "pool_w": np.ascontiguousarray(a["pool_w"]),
        "counts": counts,
        "w_mem": tiled(a["w_mem_kv"]),
        "w_out": tiled(a["w_out"]),
        "final_g": np.ascontiguousarray(a["final_g"]),
    }
    nc = bacc.Bacc("TRN2", target_bir_lowering=False, num_devices=1)
    args = [nc.dram_tensor(f"in_{n}", x.shape, mybir.dt.from_np(x.dtype), kind="ExternalInput").ap()
            for n, x in arrays.items()]
    out = nc.dram_tensor("out", (T, D), F32, kind="ExternalOutput").ap()
    hybrid_block(nc, *args, out)
    r = run_bass_kernel_spmd(nc, [{f"in_{n}": x for n, x in arrays.items()}], core_ids=[0])
    return r.results[0]["out"].reshape(a["x"].shape)
```

```python
from contextlib import ExitStack

import numpy as np

import concourse.bass as bass
from concourse import mybir

ALU = mybir.AluOpType
ACT = mybir.ActivationFunctionType
AX = mybir.AxisListType
F32 = mybir.dt.float32
F16 = mybir.dt.float16
I32 = mybir.dt.int32
BF16 = mybir.dt.bfloat16
RMAX = bass.bass_isa.ReduceOp.absmax

P = 128
D = 1024
KT = D // P
TB = 256
NT = TB // P
CHUNK = 64
NC = TB // CHUNK
HEADS = 4
DK = 64
DV = 128
RANK = 16
NPAIR = HEADS // 2
NMEM = 256
MT = NMEM // P
HALO = 16
EPS = 1e-6
NORMALIZER = 16.0
QSCALE = DK ** -0.5
MSCALE = 64 ** -0.5

CQ, CK, CV, CG, CU, CGP, CGM, CQM, CLR = 0, 256, 512, 1024, 1536, 1792, 2048, 2304, 2560
DIN = CLR + RANK
WIDE = CLR

TOP = 14
EXP_MASK = 0x7F800000
SCALE_FIELD = float((127 + TOP + 127) << 23)
INV_FIELD = float(-(TOP << 23))
TINY = 2.0 ** -100
XBITS = 10

MEM_AFTER = 5
EXP_LN = "natural_log_exp_and_others"

O_X, O_XN, O_MIX, O_T, O_U, O_QB = 0, 8192, 16384, 24576, 33024, 35200
O_KD, O_KE, O_V, O_WO, O_GATE = 39296, 41344, 43392, 47488, 80256
O_MHL, O_KAB, O_ST, O_S, O_Y, O_QM, O_END = 88448, 96640, 100736, 104832, 109952, 114048, 116096
O_TAIL = DIN * KT * 4


def hybrid_block(nc, xt, x, memt, w_in, w_ut, w_gk_up, vecs, pool_w, counts, w_mem, w_out, final_g, out):
    NB = xt.shape[0]
    ctx = ExitStack()
    with ctx:
        def sb(name, shape, dt):
            return ctx.enter_context(nc.sbuf_tensor(name, shape, dt))

        def sem(name):
            return ctx.enter_context(nc.semaphore(name))

        whl = sb("whl", [P, 2, KT, WIDE], F16)
        wlr = sb("wlr", [P, KT, 2 * RANK], F16)
        arena = sb("arena", [P, O_END // 4], F32)
        ident = sb("ident", [P, P], F32)
        ident16 = sb("ident16", [P, P], F16)
        ones = sb("ones", [P, P], F32)
        causal = sb("causal", [P, P], F32)
        keep = sb("keep", [P, TB], BF16)
        fg = sb("fg", [P, D], F32)
        kmt = sb("kmt", [P, NPAIR, 2, NMEM], F32)
        vm = sb("vm", [P, 2, MT, 256], F16)
        up2 = sb("up2", [2 * RANK, 256], F32)
        cnt = sb("cnt", [P, 2, HALO], F32)
        vec = sb("vec", [P, 32], F32)
        eps = sb("eps", [P, 2], F32)
        sca = sb("sca", [P, 24], F32)
        dec = sb("dec", [P, NPAIR, NC], F32)
        mx = sb("mx", [P, 8], F32)
        nm = sb("nm", [P, 8], F32)
        psum_p = sb("psum_p", [P, 8], F32)
        rsum = sb("rsum", [P, 8], F32)
        ysum = sb("ysum", [P, 2], F32)
        yr = sb("yr", [P, 2], F32)
        mmax = sb("mmax", [P, 4], F32)
        wmx = sb("wmx", [P, 2, KT], F32)
        idle = sb("idle", [P, 3], F32)

        g_in, g_mem, b_gk, g_out = vec[:, 0:8], vec[:, 8:16], vec[:, 16:18], vec[:, 18:26]

        def view(off, shape, dt):
            size = int(np.prod(shape)) * (2 if dt in (F16, BF16) else 4)
            ap = arena[:, off // 4:(off + size) // 4]
            if dt != F32:
                ap = ap.bitcast(dt)
            if len(shape) == 2:
                ap = ap.rearrange("p (a b) -> p a b", b=shape[1])
            if len(shape) == 3:
                ap = ap.rearrange("p (a b c) -> p a b c", b=shape[1], c=shape[2])
            if len(shape) == 4:
                ap = ap.rearrange("p (a b c d) -> p a b c d", b=shape[1], c=shape[2], d=shape[3])
            return ap

        xb = view(O_X, [KT, TB], F32)
        xn = view(O_XN, [2, KT, TB], F16)
        mixed = view(O_MIX, [KT, TB], F32)
        sq = view(O_MIX, [KT, TB], F32)
        ta = view(O_T, [2, TB], F32)
        tm = view(O_T + 2048, [2, TB], F32)
        tb = view(O_T + 4096, [2, TB], F32)
        te = view(O_T + 6144, [2, TB], F32)
        lrs = view(O_KE, [TB], F32)
        s2 = view(O_T, [2, HALO + TB], F32)
        s4 = view(O_T + 2176, [2, HALO + TB], F32)
        junk = view(O_QM, [D], BF16)
        pr = [view(O_T + 2048 * b, [2, NMEM], F32) for b in range(2)]
        phl = [view(O_T + 4096 + 2048 * b, [2, 2, NMEM], F16) for b in range(2)]
        ub = view(O_U, [2, HALO + TB], F32)
        qb = view(O_QB, [NPAIR, 2, TB], F32)
        kd = view(O_KD, [NPAIR, TB], F32)
        ke = view(O_KE, [NPAIR, TB], F32)
        osq = [view(o, [2, TB], F32) for o in (O_KD, O_KE)]
        v = view(O_V, [NT, 512], F32)
        wo = view(O_WO, [2, KT, D], F16)
        gate = view(O_GATE, [KT, TB], F32)
        mhl = view(O_MHL, [2, KT, TB], F16)
        pt = view(O_XN, [NPAIR, 8, TB], F16)
        kab = view(O_KAB, [2, NT * NPAIR, P], F32)
        sT = view(O_ST, [NT, 2 * NPAIR, P], F32)
        S = view(O_S, [NC + 1, NPAIR, P], F32)
        yb = view(O_Y, [D], F32)
        qm = view(O_QM, [NPAIR, TB], F32)
        wraw = view(0, [KT, DIN], F32)
        woraw = view(O_TAIL, [KT, D], F32)
        memb = view(O_TAIL, [KT, NMEM], F32)
        wmraw = view(O_TAIL + 8192, [KT, 512], F32)
        wflat = whl[:, :, :, :].rearrange("p a b c -> p (a b c)").bitcast(F32)
        wut = wflat[:, 0:2048].rearrange("p (a b) -> p a b", a=2)
        pwb = wflat[:, 2048:2304].rearrange("p (a b) -> p a b", a=2)
        msq = wflat[:, 2304:2304 + KT * NMEM].rearrange("p (a b) -> p a b", a=KT)
        rmem = wflat[:, 4608:4608 + NMEM]
        vraw = wflat[:, 5120:5120 + 512].rearrange("p (a b) -> p a b", a=MT)

        bank = [ctx.enter_context(nc.psum_tensor(f"bank{i}", [P, 512], F32)) for i in range(8)]
        b16 = {i: bank[i][:, :].bitcast(F16) for i in (6, 7)}

        def col(n):
            return sca[:, n:n + 1]
        s_w, i_w, s_o, i_o, s_v, i_v, s_m, i_m, sc_in, sc_q, sc_out = (col(n) for n in range(11))
        gs = sca[:, 12:20]
        e_tmp = col(20)
        m_tmp = col(21)

        d_vec, d_mem, d_wut, d_wout, d_x, d_res, d_store = (
            sem(n) for n in ("d_vec", "d_mem", "d_wut", "d_wout", "d_x", "d_res", "d_store"))
        d_w = [sem(f"d_w{k}") for k in range(KT)]
        cleared, built, ident_ok, mem_sq, mem_sum, mem_ms, mem_ln, mem_r, mem_n = (
            sem(n) for n in ("cleared", "built", "ident_ok", "mem_sq", "mem_sum", "mem_ms", "mem_ln", "mem_r", "mem_n"))
        memk_done, memv_done, memk_out, memv_out, fold_done, fold_out = (
            sem(n) for n in ("memk_done", "memv_done", "memk_out", "memv_out", "fold_done", "fold_out"))
        max_in, max_all, prep, hi_w, lo_w, hi_v, hi_o, lo_o, scaled = (
            sem(n) for n in ("max_in", "max_all", "prep", "hi_w", "lo_w", "hi_v", "hi_o", "lo_o", "scaled"))
        low_rank = sem("low_rank")
        pe_lr, pe_q, pe_k, pe_logit, pe_v, pe_p2, pe_out, pe_ket, pe_sc, pe_ms, pe_st, pe_rb, pe_pt, pe_o, pe_msq, pe_pv = (
            sem(n) for n in ("pe_lr", "pe_q", "pe_k", "pe_logit", "pe_v", "pe_p2", "pe_out", "pe_ket", "pe_sc",
                             "pe_ms", "pe_st", "pe_rb", "pe_pt", "pe_o", "pe_msq", "pe_pv"))
        lr_out, abs_ok, expabs, softplus, eb_ok, enb_ok, ebl_ok, v_out, p2_out, y_sq, y_ln, y_r, x_sq = (
            sem(n) for n in ("lr_out", "abs_ok", "expabs", "softplus", "eb_ok", "enb_ok", "ebl_ok", "v_out",
                             "p2_out", "y_sq", "y_ln", "y_r", "x_sq"))
        ket_out, p_exp, p_hi, rb_ln, rb_ok, x_hi, o_sq, o_ln, o_r, m_hi = (
            sem(n) for n in ("ket_out", "p_exp", "p_hi", "rb_ln", "rb_ok", "x_hi", "o_sq", "o_ln", "o_r", "m_hi"))
        z_ok, gk_ok, b_ok, bl_ok, q_ok, dec_ok, kd_ok, ke_ok, pooled, y_add, y_ok = (
            sem(n) for n in ("z_ok", "gk_ok", "b_ok", "bl_ok", "q_ok", "dec_ok", "kd_ok", "ke_ok", "pooled",
                             "y_add", "y_ok"))
        sT_ok, max_ok, nmax_ok, rs_ok, pn_ok, s_ok, pt_out, xn_ok, og_ok, mix_g, mix_m, mix_p, mmax_ok, m_sc, m_lo = (
            sem(n) for n in ("sT_ok", "max_ok", "nmax_ok", "rs_ok", "pn_ok", "s_ok", "pt_out", "xn_ok", "og_ok",
                             "mix_g", "mix_m", "mix_p", "mmax_ok", "m_sc", "m_lo"))
        w_sum, halo_ok, sq_add, p_lo, x_lo, m_all, s_carry = (
            sem(n) for n in ("w_sum", "halo_ok", "sq_add", "p_lo", "x_lo", "m_all", "s_carry"))

        block = ctx.enter_context(nc.Block())

        def wait_split(eng, k):
            eng.wait_ge(hi_w, k + 1)
            eng.wait_ge(lo_w, k + 1)

        def run_blocks(eng, step, tail):
            step(0, True, False)
            with eng.Fori(1, NB - 1) as i:
                step(i, False, False)
            step(NB - 1, False, True)
            tail(NB)

        @block.sync
        def _(sp):
            sp.dma_start(vec[:, 0:26], vecs).then_inc(d_vec, 16)
            sp.dma_start(cnt[:, :, :], counts).then_inc(d_vec, 16)
            sp.dma_start(up2[0:RANK, :], w_gk_up).then_inc(d_vec, 16)
            sp.dma_start(up2[RANK:2 * RANK, :], w_gk_up).then_inc(d_vec, 16)
            sp.dma_start(fg[:, :], final_g.partition_broadcast(P)).then_inc(d_vec, 16)
            sp.dma_start(memb, memt).then_inc(d_mem, 16)
            sp.dma_start(wmraw, w_mem).then_inc(d_mem, 16)
            sp.dma_start(wut, w_ut).then_inc(d_wut, 16)
            sp.wait_ge(cleared, 1)
            for g in range(4):
                h = g % 2
                sp.dma_start(pwb[64 * h:64 * h + 64, g // 2, 64 * h:64 * h + 64], pool_w[g]).then_inc(d_wut, 16)
            for k in range(KT):
                sp.dma_start(wraw[:, k, 0:CU], w_in[:, k, 0:CU]).then_inc(d_w[k], 16)
                sp.dma_start(wraw[:, k, CGP:DIN], w_in[:, k, CU:DIN - 256]).then_inc(d_w[k], 16)
            sp.wait_ge(memk_done, 1)
            sp.wait_ge(memv_done, 1)
            sp.dma_start(woraw, w_out).then_inc(d_wout, 16)
            wait_split(sp, 0)
            sp.dma_start(xb, xt[0]).then_inc(d_x, 16)

            def outputs(j, t):
                rows = bass.ds(j * TB + t * P, P)
                if isinstance(j, int) and j == 0 and t == 0:
                    sp.wait_ge(lo_o, KT)
                    sp.wait_ge(hi_o, KT)
                else:
                    sp.wait_ge(d_store, (j * NT + t) * 16)
                sp.dma_start(yb, x[rows, :]).then_inc(d_res, 16)
                sp.wait_ge(y_ok, j * NT + t + 1)
                sp.dma_start(out[rows, :], yb).then_inc(d_store, 16)

            def step(i, first, last):
                if not last:
                    sp.wait_ge(x_hi, 2 * (i + 1))
                    sp.wait_ge(x_lo, 2 * (i + 1))
                    sp.dma_start(xb, xt[i + 1] if first else xt[bass.ds(i + 1, 1)].rearrange(
                        "a p k t -> (a p) k t")).then_inc(d_x, 16)
                if not first:
                    for t in range(NT):
                        outputs(i - 1, t)

            def tail(n):
                for t in range(NT):
                    outputs(n - 1, t)
                sp.wait_ge(d_store, 16 * NT * n)

            run_blocks(sp, step, tail)

        @block.tensor
        def _(pe):
            pe.wait_ge(d_wut, 16 * 5)
            for k in range(KT):
                for g in range(2):
                    mm = nc.tensor.matmul(bank[4 + k // 2][:, (k % 2) * 256 + g * P:(k % 2) * 256 + g * P + P],
                                          wut[:, g, k * P:(k + 1) * P], pwb[:, g, :], start=True, stop=True)
            mm.then_inc(fold_done, 1)
            pe.wait_ge(built, 3)
            pe.wait_ge(mem_sum, 3)
            nc.tensor.matmul(bank[0][:, 0:NMEM], ones[:, :], msq[:, 0, :], start=True, stop=True).then_inc(mem_ms, 1)
            pe.wait_ge(mem_n, KT)
            for j in range(2):
                for k in range(KT):
                    mm = nc.tensor.matmul(bank[1][:, j * NMEM:(j + 1) * NMEM], wmraw[:, k, j * P:(j + 1) * P],
                                          memb[:, k, :], start=k == 0, stop=k == KT - 1)
            mm.then_inc(memk_done, 1)
            for j in range(MT):
                for k in range(KT):
                    mm = nc.tensor.matmul(bank[2][:, j * 256:(j + 1) * 256], memb[:, k, j * P:(j + 1) * P],
                                          wmraw[:, k, 256:512], start=k == 0, stop=k == KT - 1)
            mm.then_inc(memv_done, 1)

            def rms_sum(n):
                pe.wait_ge(sq_add, 3 * (n + 1))
                nc.tensor.matmul(bank[3][:, 0:TB], ones[:, :], sq[:, 0, :], start=True, stop=True).then_inc(pe_rb, 1)

            pe.wait_ge(memk_out, 2)
            rms_sum(0)

            def split(ap, tiles, parts):
                last = (tiles - 1, 2)
                for k in range(tiles):
                    for n, (a, b) in enumerate(((0, 0), (0, 1), (1, 0))):
                        lhs, rhs = parts(k, a, b)
                        mm = nc.tensor.matmul(ap, lhs, rhs, start=k == 0 and n == 0, stop=(k, n) == last)
                return mm

            def features(b, c0):
                for j in range(2):
                    c = c0 + j * P
                    mm = split(bank[b][:, j * TB:(j + 1) * TB], KT,
                               lambda k, p, r, c=c: (whl[:, p, k, c:c + P], xn[:, r, k, :]))
                return mm

            def out_proj(j, n):
                t, h = n // 2, n % 2
                if n == 0:
                    pe.wait_ge(m_hi, j + 1)
                    pe.wait_ge(m_lo, j + 1)
                if n >= 2:
                    pe.wait_ge(y_add, 4 * j + n + 3)
                split(bank[h][:, :], KT, lambda k, p, r: (mhl[:, p, k, t * P:(t + 1) * P],
                                                          wo[:, r, k, h * 512:(h + 1) * 512])).then_inc(pe_out, 1)

            def bank_free(i, first, b):
                if first:
                    return
                pe.wait_ge(y_add, 4 * i - 1 + b)

            def step(i, first, last):
                if first:
                    wait_split(pe, KT - 1)
                    pe.wait_ge(low_rank, 3)
                pe.wait_ge(x_hi, 2 * (i + 1))
                pe.wait_ge(x_lo, 2 * (i + 1))
                bank_free(i, first, 0)
                for r in range(2):
                    for k in range(KT):
                        mm = nc.tensor.matmul(bank[0][0:2 * RANK, 0:TB], wlr[:, k, :], xn[:, r, k, :],
                                              start=r == 0 and k == 0, stop=r == 1 and k == KT - 1)
                mm.then_inc(pe_lr, 1)
                bank_free(i, first, 1)
                features(1, CQ).then_inc(pe_q, 1)
                pe.wait_ge(rb_ok, i + 1)
                pe.wait_ge(lr_out, i + 1)
                for j in range(2):
                    mm = nc.tensor.matmul(bank[3][:, j * TB:(j + 1) * TB], up2[:, j * P:(j + 1) * P],
                                          lrs[0:2 * RANK, :], start=True, stop=True)
                mm.then_inc(pe_logit, 1)
                if not first:
                    pe.wait_ge(mix_m, i)
                features(2, CK).then_inc(pe_k, 1)
                for t in range(NT):
                    if t == 1:
                        pe.wait_ge(q_ok, 2 * (i + 1))
                    split(bank[t][:, :], KT, lambda k, p, r: (xn[:, p, k, t * P:(t + 1) * P],
                                                               whl[:, r, k, CV:CV + 512])).then_inc(pe_v, 1)
                pe.wait_ge(ke_ok, i + 1)
                features(2, CG).then_inc(pe_p2, 1)
                pe.wait_ge(z_ok, 2 * (i + 1))
                features(3, CG + 256).then_inc(pe_p2, 1)
                for n, c in enumerate((CU, CGP, CGM, CQM)):
                    if n < 2:
                        pe.wait_ge(v_out, 2 * i + n + 1)
                    else:
                        pe.wait_ge(p2_out, 6 * i + n - 1)
                    features(n, c).then_inc(pe_p2, 1)
                pe.wait_ge(ke_ok, i + 1)
                if not first:
                    pe.wait_ge(mix_g, 2 * i)
                else:
                    pe.wait_ge(fold_out, 4)
                for t in range(NT):
                    for p in range(NPAIR):
                        n = t * NPAIR + p
                        mm = nc.tensor.transpose(bank[4][:, n * P:(n + 1) * P], ke[:, p, t * P:(t + 1) * P],
                                                 ident[:, :])
                mm.then_inc(pe_ket, 1)
                pe.wait_ge(kd_ok, i + 1)
                pe.wait_ge(q_ok, 2 * (i + 1))
                for t in range(NT):
                    if not first:
                        pe.wait_ge(pt_out, 4 * i - 1 + t)
                    for p in range(NPAIR):
                        mm = nc.tensor.matmul(bank[6 + t][:, p * 256:(p + 1) * 256], kd[:, p, t * P:(t + 1) * P],
                                              qb[:, p, :, t * P:(t + 1) * P], start=True, stop=True)
                    mm.then_inc(pe_sc, 1)

                def mem_scores(n):
                    t, p, b = n // NPAIR, n % NPAIR, 2 + n % 2
                    if n < 2:
                        pe.wait_ge(p2_out, 6 * (i + 1))
                    else:
                        pe.wait_ge(p_exp, 4 * i + n - 1)
                    nc.tensor.matmul(bank[b][:, :], qm[:, p, t * P:(t + 1) * P], kmt[:, p, :, :],
                                     start=True, stop=True).then_inc(pe_ms, 1)

                def state(c, b):
                    t, odd = c // 2, c % 2
                    for p in range(NPAIR):
                        mm = nc.tensor.matmul(bank[b][:, p * 256:(p + 1) * 256], kab[:, odd, t * NPAIR + p, :],
                                              v[:, t, p * 256:(p + 1) * 256], start=True, stop=True)
                    mm.then_inc(pe_st, 1)

                def turn_p(n, b):
                    pe.wait_ge(p_hi, 4 * i + n + 1)
                    pe.wait_ge(p_lo, 4 * i + n + 1)
                    for h in range(2):
                        for m in range(MT):
                            for r in range(2):
                                j = (h * MT + m) * 2 + r
                                mm = nc.tensor.transpose(b16[b][:, j * P:(j + 1) * P],
                                                         phl[n % 2][:, r, h, m * P:(m + 1) * P], ident16[:, :])
                    mm.then_inc(pe_pt, 1)

                def head_out(p, b):
                    for t in range(NT):
                        for h in range(2):
                            nc.tensor.matmul(bank[b][:, h * TB + t * P:h * TB + (t + 1) * P],
                                             v[:, t, (2 * p + h) * DV:(2 * p + h + 1) * DV],
                                             sT[:, t, 2 * p + h, :], start=t == 0 and h == 0, stop=False,
                                             skip_group_check=True)
                    o3 = bank[b][:, :].rearrange("p (h t) -> p h t", h=2)
                    for c in range(NC):
                        mm = nc.tensor.matmul(o3[:, :, c * CHUNK:(c + 1) * CHUNK], S[:, c, p, :],
                                              qb[:, p, :, c * CHUNK:(c + 1) * CHUNK], start=False,
                                              stop=c == NC - 1, skip_group_check=True)
                    mm.then_inc(pe_o, 1)

                def head_ms(p):
                    pe.wait_ge(o_sq, 2 * i + p + 1)
                    nc.tensor.matmul(bank[6 + p][:, :], ones[:, :], osq[p], start=True,
                                     stop=True).then_inc(pe_msq, 1)

                def quarter(n):
                    if not first:
                        if n < 2:
                            pe.wait_ge(p2_out, 6 * i + 3 + n)
                        out_proj(i - 1, n)

                mem_scores(0)
                mem_scores(1)
                quarter(0)
                pe.wait_ge(ket_out, 2 * (i + 1))
                pe.wait_ge(v_out, 2 * (i + 1))
                state(0, 5)
                state(1, 4)
                mem_scores(2)
                mem_scores(3)
                pe.wait_ge(sT_ok, 2 * i + 1)
                turn_p(0, 6)
                quarter(1)
                pe.wait_ge(s_ok, 4 * i + 1)
                state(2, 5)
                pe.wait_ge(sT_ok, 2 * i + 2)
                turn_p(1, 7)
                pe.wait_ge(s_ok, 4 * i + 2)
                state(3, 4)
                pe.wait_ge(pt_out, 4 * i + 1)
                turn_p(2, 6)
                quarter(2)
                if not last:
                    pe.wait_ge(p_exp, 4 * i + 4)
                    rms_sum(i + 1)
                pe.wait_ge(pt_out, 4 * i + 2)
                turn_p(3, 7)
                pe.wait_ge(s_ok, 4 * i + 3)
                head_out(0, 5)
                pe.wait_ge(s_ok, 4 * i + 4)
                head_out(1, 4)
                pe.wait_ge(pt_out, 4 * i + 4)
                pe.wait_ge(p_exp, 4 * i + 3)
                for h in range(HEADS):
                    p, r0 = h // 2, 64 * (h % 2)
                    ps = bank[2][r0:r0 + 64, p * TB:(p + 1) * TB]
                    for m in range(MT):
                        for n, (a, b) in enumerate(((0, 0), (0, 1), (1, 0))):
                            mm = nc.tensor.matmul(ps, vm[:, a, m, h * 64:(h + 1) * 64],
                                                  pt[:, p, ((h % 2) * MT + m) * 2 + b, :],
                                                  start=m == 0 and n == 0, stop=m == MT - 1 and n == 2)
                mm.then_inc(pe_pv, 1)
                quarter(3)
                head_ms(0)
                head_ms(1)

            def tail(n):
                for b in range(4):
                    if b < 2:
                        bank_free(n, False, b)
                    out_proj(n - 1, b)

            run_blocks(pe, step, tail)

        @block.scalar
        def _(act):
            nc.scalar.preload_act_table_set(EXP_LN)
            act.wait_ge(d_mem, 32)
            nc.scalar.activation(msq, memb, ACT.Square).then_inc(mem_sq, 1)
            act.wait_ge(fold_done, 1)
            for n in range(4):
                nc.scalar.activation(wraw[:, 2 * n:2 * n + 2, CU:CU + 256],
                                     bank[4 + n][:, :].rearrange("p (a b) -> p a b", a=2), ACT.Copy).then_inc(fold_out, 1)
            act.wait_ge(mem_ms, 1)
            act.wait_ge(built, 3)
            nc.scalar.activation(rmem, bank[0][:, 0:NMEM], ACT.Ln, bias=eps[:, 0:1], scale=1.0 / D).then_inc(mem_ln, 1)
            act.wait_ge(mem_ln, 1)
            nc.scalar.activation(rmem, rmem, ACT.Exp, scale=-0.5).then_inc(mem_r, 1)
            act.wait_ge(memk_done, 1)
            act.wait_ge(cleared, 2)
            for h in range(2):
                r = slice(64 * h, 64 * h + 64)
                nc.scalar.activation(kmt[r, :, h, :], bank[1][r, :].rearrange("p (a b) -> p a b", a=2),
                                     ACT.Copy).then_inc(memk_out, 1)
            act.wait_ge(memv_done, 1)
            nc.scalar.activation(vraw, bank[2][:, :].rearrange("p (a b) -> p a b", a=MT), ACT.Copy).then_inc(memv_out, 1)
            act.wait_ge(scaled, 2)
            nc.scalar.activation(vm[:, 0, :, :], vraw, ACT.Copy, scale=s_v).then_inc(hi_v, 1)

            def hi_tile(k):
                if k == 4:
                    act.wait_ge(prep, 1)
                nc.scalar.activation(whl[:, 0, k, :], wraw[:, k, 0:WIDE], ACT.Copy, scale=gs[:, k:k + 1]).then_inc(hi_w, 1)

            def squares(n):
                act.wait_ge(d_x, 16 * (n + 1))
                nc.scalar.activation(sq, xb, ACT.Square).then_inc(x_sq, 1)

            def rstd(n):
                act.wait_ge(pe_rb, n + 1)
                nc.scalar.activation(sq[:, 1, :], bank[3][:, 0:TB], ACT.Ln, bias=eps[:, 0:1],
                                     scale=1.0 / D).then_inc(rb_ln, 1)
                act.wait_ge(rb_ln, n + 1)
                nc.scalar.activation(sq[:, 1, :], sq[:, 1, :], ACT.Exp, bias=eps[:, 1:2],
                                     scale=-0.5).then_inc(rb_ok, 1)

            def x_parts(n):
                act.wait_ge(xn_ok, n + 1)
                if not isinstance(n, int) or n:
                    act.wait_ge(pe_pv, n)
                for h in range(2):
                    k = slice(h * KT // 2, (h + 1) * KT // 2)
                    nc.scalar.activation(xn[:, 0, k, :], xb[:, k, :], ACT.Copy).then_inc(x_hi, 1)

            for k in range(5):
                hi_tile(k)
            wait_split(act, 2)
            act.wait_ge(low_rank, 3)
            squares(0)
            for k in range(5, KT):
                hi_tile(k)
            rstd(0)
            x_parts(0)

            def mixed_hi(n):
                act.wait_ge(m_sc, n + 1)
                nc.scalar.activation(mhl[:, 0, :, :], mixed, ACT.Copy, scale=s_m).then_inc(m_hi, 1)

            def norm_y(j, t):
                act.wait_ge(y_add, 4 * (j + 1) + 2 * t + 2)
                act.wait_ge(pe_ms, 4 * (j + 1))
                nc.scalar.activation(junk, yb, ACT.Square, accum_out=ysum[:, 0:1]).then_inc(y_sq, 1)
                act.wait_ge(y_sq, 2 * j + t + 1)
                nc.scalar.activation(yr[:, 1:2], ysum[:, 0:1], ACT.Ln, bias=eps[:, 0:1],
                                     scale=1.0 / D).then_inc(y_ln, 1)
                act.wait_ge(y_ln, 2 * j + t + 1)
                nc.scalar.activation(yr[:, 0:1], yr[:, 1:2], ACT.Exp, scale=-0.5).then_inc(y_r, 1)

            def step(i, first, last):
                act.wait_ge(pe_lr, i + 1)
                if not first:
                    act.wait_ge(mix_g, 2 * i)
                nc.scalar.activation(lrs[0:2 * RANK, :], bank[0][0:2 * RANK, 0:TB], ACT.Copy,
                                     scale=sc_in[0:2 * RANK, :]).then_inc(lr_out, 1)
                act.wait_ge(z_ok, 2 * (i + 1))
                nc.scalar.activation(ta, tm, ACT.Abs).then_inc(abs_ok, 1)
                act.wait_ge(abs_ok, i + 1)
                nc.scalar.activation(ta, ta, ACT.Exp, scale=-1.0).then_inc(expabs, 1)
                act.wait_ge(expabs, i + 1)
                nc.scalar.activation(ta, ta, ACT.Ln, bias=1.0).then_inc(softplus, 1)
                act.wait_ge(b_ok, 2 * (i + 1))
                nc.scalar.activation(te, tb, ACT.Exp, scale=1.0 / NORMALIZER).then_inc(eb_ok, 1)
                nc.scalar.activation(ta, tb, ACT.Exp, scale=-1.0 / NORMALIZER).then_inc(enb_ok, 1)
                act.wait_ge(bl_ok, i + 1)
                nc.scalar.activation(tm, tm, ACT.Exp, scale=1.0 / NORMALIZER).then_inc(ebl_ok, 1)
                if first:
                    act.wait_ge(scaled, 3)
                    for k in range(KT):
                        nc.scalar.activation(wo[:, 0, k, :], woraw[:, k, :], ACT.Copy,
                                             scale=g_out[:, k:k + 1]).then_inc(hi_o, 1)
                for t in range(NT):
                    act.wait_ge(pe_v, 2 * i + t + 1)
                    nc.scalar.activation(v[:, t, :], bank[t][:, :], ACT.Copy, scale=sc_in).then_inc(v_out, 1)
                    if t == 0 and not first:
                        mixed_hi(i - 1)
                if first:
                    act.wait_ge(lo_o, KT)
                    act.wait_ge(hi_o, KT)

                def silu(n, b, g):
                    act.wait_ge(pe_p2, 6 * i + n)
                    nc.scalar.activation(gate[:, g:g + 2, :], bank[b][:, :].rearrange("p (a t) -> p a t", a=2),
                                         ACT.Silu, scale=sc_in).then_inc(p2_out, 1)

                silu(1, 2, 0)
                silu(2, 3, 2)
                act.wait_ge(pe_p2, 6 * i + 3)
                act.wait_ge(halo_ok, i + 1)
                nc.scalar.activation(ub[:, :, HALO:], bank[0][:, :].rearrange("p (a t) -> p a t", a=2), ACT.Copy,
                                     scale=sc_in).then_inc(p2_out, 1)
                silu(4, 1, 4)
                silu(5, 2, 6)
                nc.scalar.preload_act_table_set(EXP_LN)
                act.wait_ge(pe_p2, 6 * i + 6)
                if not first:
                    act.wait_ge(y_sq, 2 * (i - 1))
                nc.scalar.activation(qm, bank[3][:, :].rearrange("p (a t) -> p a t", a=2), ACT.Copy,
                                     scale=sc_in).then_inc(p2_out, 1)
                if not last:
                    if not first:
                        act.wait_ge(m_lo, i)
                    squares(i + 1)
                act.wait_ge(pe_ket, i + 1)
                if first:
                    act.wait_ge(cleared, 4)
                for odd in range(2):
                    r = slice(64 * odd, 64 * odd + 64)
                    nc.scalar.activation(kab[r, odd, :, :], bank[4][r, :].rearrange("p (a b) -> p a b", b=P),
                                         ACT.Copy).then_inc(ket_out, 1)

                def p_exp_of(n):
                    act.wait_ge(nmax_ok, 4 * i + n + 1)
                    if n >= 2:
                        act.wait_ge(p_lo, 4 * i + n - 1)
                    else:
                        act.wait_ge(pooled, 4 * (i + 1))
                        if not first:
                            act.wait_ge(pe_pt, 4 * i)
                    for h in range(2):
                        a = nc.scalar.activation(pr[n % 2][:, h, :], bank[2 + n % 2][:, h * 256:(h + 1) * 256], ACT.Exp,
                                                 bias=nm[:, 2 * n + h:2 * n + h + 1], scale=MSCALE,
                                                 accum_out=psum_p[:, 2 * n + h:2 * n + h + 1])
                    a.then_inc(p_exp, 1)

                def p_hi_of(n):
                    act.wait_ge(pn_ok, 4 * i + n + 1)
                    if n >= 2:
                        act.wait_ge(pe_pt, 4 * i + n - 1)
                    nc.scalar.activation(phl[n % 2][:, 0, :, :], pr[n % 2], ACT.Copy).then_inc(p_hi, 1)

                p_exp_of(0)
                p_exp_of(1)
                p_hi_of(0)
                p_hi_of(1)
                p_exp_of(2)
                p_exp_of(3)
                p_hi_of(2)
                if not first:
                    norm_y(i - 1, 0)
                p_hi_of(3)
                if not last:
                    rstd(i + 1)

                for p, b in ((0, 5), (1, 4)):
                    act.wait_ge(pe_o, 2 * i + p + 1)
                    nc.scalar.activation(osq[p], bank[b][:, :].rearrange("p (a t) -> p a t", a=2),
                                         ACT.Square).then_inc(o_sq, 1)
                if not last:
                    x_parts(i + 1)
                for p in range(NPAIR):
                    act.wait_ge(pe_msq, 2 * i + p + 1)
                    nc.scalar.activation(osq[p], bank[6 + p][:, :].rearrange("p (a t) -> p a t", a=2), ACT.Ln,
                                         bias=eps[:, 0:1], scale=1.0 / DV).then_inc(o_ln, 1)
                    act.wait_ge(o_ln, 2 * i + p + 1)
                    nc.scalar.activation(osq[p], osq[p], ACT.Exp, scale=-0.5).then_inc(o_r, 1)
                if not first:
                    norm_y(i - 1, 1)

            def tail(n):
                mixed_hi(n - 1)
                norm_y(n - 1, 0)
                norm_y(n - 1, 1)

            run_blocks(act, step, tail)

        @block.vector
        def _(dve):
            nc.vector.memset(pwb, 0.0).then_inc(cleared, 1)
            nc.vector.memset(kmt[:, :, :, :], 0.0).then_inc(cleared, 1)
            nc.vector.memset(keep[:, :], 1.0).then_inc(gk_ok, 1)
            dve.wait_ge(gk_ok, 1)
            nc.vector.memset(keep[:, 0:TB:CHUNK], 0.0).then_inc(gk_ok, 1)

            steps = [0]

            def after(ins):
                steps[0] += 1
                ins.then_inc(max_in, 1)
                dve.wait_ge(max_in, steps[0])

            def exponents(src, s, inv):
                after(nc.vector.tensor_scalar(m_tmp, src, TINY, None, ALU.max))
                after(nc.vector.tensor_scalar(e_tmp.bitcast(I32), m_tmp.bitcast(I32), EXP_MASK, None, ALU.bitwise_and))
                nc.vector.tensor_scalar(s.bitcast(I32), e_tmp.bitcast(I32), -1.0, SCALE_FIELD, ALU.mult, ALU.add)
                after(nc.vector.tensor_scalar(inv.bitcast(I32), e_tmp.bitcast(I32), INV_FIELD, None, ALU.add))

            def normalise(n):
                dve.wait_ge(rb_ok, n + 1)
                r = sq[:, 1:2, :].broadcast_to([P, KT, TB])
                nc.vector.tensor_tensor(xb, xb, r, ALU.mult).then_inc(xn_ok, 1)

            dve.wait_ge(d_vec, 16 * 5)
            dve.wait_ge(fold_out, 4)
            for k in range(KT):
                if k == 0:
                    dve.wait_ge(mem_r, 1)
                    for m in range(KT):
                        nc.vector.scalar_tensor_tensor(memb[:, m, :], memb[:, m, :], g_mem[:, m:m + 1], rmem,
                                                       ALU.mult, ALU.mult).then_inc(mem_n, 1)
                dve.wait_ge(d_w[k], 32)
                a = nc.vector.tensor_reduce(wmx[:, 0, k:k + 1], wraw[:, k, :], AX.X, ALU.max, apply_absolute_value=True)
                if k == MEM_AFTER:
                    dve.wait_ge(memv_out, 1)
                    after(nc.vector.tensor_reduce(mmax[:, 0:1], vraw, AX.XY, ALU.max, apply_absolute_value=True))
                    nc.vector.tensor_copy(mmax[:, 1:2], mmax[:, 0:1]).then_inc(mmax_ok, 1)
                if k == MEM_AFTER + 1:
                    dve.wait_ge(max_all, 1)
                    exponents(mmax[:, 2:3], s_v, i_v)
                    nc.vector.tensor_copy(mmax[:, 3:4], mmax[:, 2:3]).then_inc(scaled, 1)
            after(a)
            after(nc.vector.tensor_tensor(wmx[:, 0, :], wmx[:, 0, :], g_in, ALU.mult))
            nc.vector.tensor_reduce(mmax[:, 1:2], wmx[:, 0, :], AX.X, ALU.max,
                                    apply_absolute_value=True).then_inc(mmax_ok, 1)
            dve.wait_ge(max_all, 2)
            exponents(mmax[:, 2:3], s_w, i_w)
            nc.vector.tensor_scalar(sc_q, i_w, 2.0 ** -XBITS * QSCALE, None, ALU.mult)
            nc.vector.tensor_scalar(sc_in, i_w, 2.0 ** -XBITS, None, ALU.mult)
            nc.vector.tensor_scalar(gs, g_in, s_w, None, ALU.mult).then_inc(scaled, 1)
            dve.wait_ge(hi_v, 1)
            nc.vector.scalar_tensor_tensor(vm[:, 1, :, :], vraw, s_v, vm[:, 0, :, :], ALU.mult,
                                           ALU.subtract).then_inc(prep, 1)
            dve.wait_ge(scaled, 2)
            for k in range(KT):
                dve.wait_ge(hi_w, k + 1)
                nc.vector.scalar_tensor_tensor(whl[:, 1, k, :], wraw[:, k, 0:WIDE], gs[:, k:k + 1],
                                               whl[:, 0, k, :], ALU.mult, ALU.subtract).then_inc(lo_w, 1)
                if k == KT - 2:
                    normalise(0)

            dve.wait_ge(d_wout, 16)
            for k in range(KT):
                a = nc.vector.tensor_reduce(wmx[:, 1, k:k + 1], woraw[:, k, :], AX.X, ALU.max, apply_absolute_value=True)
            after(a)
            after(nc.vector.tensor_tensor(wmx[:, 1, :], wmx[:, 1, :], g_out, ALU.mult))
            nc.vector.tensor_reduce(mmax[:, 1:2], wmx[:, 1, :], AX.X, ALU.max,
                                    apply_absolute_value=True).then_inc(mmax_ok, 1)
            dve.wait_ge(max_all, 3)
            exponents(mmax[:, 2:3], s_o, i_o)
            after(nc.vector.tensor_scalar(g_out, g_out, s_o, None, ALU.mult))
            nc.vector.tensor_copy(mmax[:, 3:4], mmax[:, 2:3]).then_inc(scaled, 1)

            def mixed_lo(n):
                dve.wait_ge(m_all, n + 1)
                nc.vector.tensor_scalar(m_tmp, mmax[:, 2:3], TINY, None, ALU.max).then_inc(m_tiny, 1)
                dve.wait_ge(m_tiny, n + 1)
                nc.vector.tensor_scalar(e_tmp.bitcast(I32), m_tmp.bitcast(I32), EXP_MASK, None,
                                        ALU.bitwise_and).then_inc(m_exp, 1)
                dve.wait_ge(m_exp, n + 1)
                nc.vector.tensor_scalar(i_m.bitcast(I32), e_tmp.bitcast(I32), INV_FIELD, None,
                                        ALU.add).then_inc(m_inv, 1)
                nc.vector.tensor_scalar(s_m.bitcast(I32), e_tmp.bitcast(I32), -1.0, SCALE_FIELD, ALU.mult,
                                        ALU.add).then_inc(m_sc, 1)
                dve.wait_ge(m_inv, n + 1)
                nc.vector.tensor_scalar(sc_out, i_m, i_o, None, ALU.mult).then_inc(sc_ok, 1)
                dve.wait_ge(m_hi, n + 1)
                nc.vector.scalar_tensor_tensor(mhl[:, 1, :, :], mixed, s_m, mhl[:, 0, :, :], ALU.mult,
                                               ALU.subtract).then_inc(m_lo, 1)

            def add_rows(j, n):
                t, h = n // 2, n % 2
                if h == 0:
                    dve.wait_ge(d_res, 16 * (NT * j + t + 1))
                dve.wait_ge(sc_ok, j + 1)
                dve.wait_ge(pe_out, 4 * j + n + 1)
                c = slice(h * 512, (h + 1) * 512)
                nc.vector.scalar_tensor_tensor(yb[:, c], bank[h][:, :], sc_out, yb[:, c], ALU.mult,
                                               ALU.add).then_inc(y_add, 1)

            def norm_rows(j, t):
                dve.wait_ge(y_add, 4 * (j + 1) + 2 * t + 2)
                dve.wait_ge(y_r, NT * j + t + 1)
                nc.vector.scalar_tensor_tensor(yb, yb, yr[:, 0:1], fg[:, :], ALU.mult, ALU.mult).then_inc(y_ok, 1)

            for n in range(4):
                nc.vector.memset(nm[:, n:n + 1], 0.0).then_inc(y_add, 1)

            def step(i, first, last):
                dve.wait_ge(pe_logit, i + 1)
                if not first:
                    dve.wait_ge(p_lo, 4 * i)
                    dve.wait_ge(pe_pt, 4 * i)
                for j in range(2):
                    nc.vector.tensor_scalar(tm[:, j, :], bank[3][:, j * TB:(j + 1) * TB], b_gk[:, j:j + 1], None,
                                            ALU.add).then_inc(z_ok, 1)
                dve.wait_ge(z_ok, 2 * (i + 1))
                dve.wait_ge(softplus, i + 1)
                nc.vector.scalar_tensor_tensor(tm, tm, 0.0, ta, ALU.min, ALU.subtract).then_inc(gk_ok, 1)
                dve.wait_ge(gk_ok, i + 3)
                for j in range(2):
                    nc.vector.tensor_tensor_scan(tb[:, j, :], keep[:, :], tm[:, j, :], 0.0, ALU.mult,
                                                 ALU.add).then_inc(b_ok, 1)
                dve.wait_ge(b_ok, 2 * (i + 1))
                b4 = tb.rearrange("p a (c t) -> p (a c) t", t=CHUNK)
                nc.vector.tensor_tensor(tm.rearrange("p a (c t) -> p (a c) t", t=CHUNK),
                                        b4[:, :, CHUNK - 1:CHUNK].broadcast_to([P, 2 * NC, CHUNK]), b4,
                                        ALU.subtract).then_inc(bl_ok, 1)
                dve.wait_ge(eb_ok, i + 1)
                dve.wait_ge(pe_q, i + 1)
                if first:
                    dve.wait_ge(cleared, 3)
                else:
                    dve.wait_ge(pe_o, 2 * i)
                for h in range(2):
                    r = slice(64 * h, 64 * h + 64)
                    nc.vector.scalar_tensor_tensor(qb[r, :, h, :], bank[1][r, :].rearrange("p (a t) -> p a t", a=2),
                                                   sc_q[r, :], te[r, :, :], ALU.mult, ALU.mult).then_inc(q_ok, 1)
                nc.vector.tensor_copy(dec[:, :, :], te[:, :, CHUNK - 1:TB:CHUNK]).then_inc(dec_ok, 1)
                dve.wait_ge(enb_ok, i + 1)
                dve.wait_ge(pe_k, i + 1)
                if not first:
                    dve.wait_ge(pe_msq, 2 * i)
                k3 = bank[2][:, :].rearrange("p (a t) -> p a t", a=2)
                nc.vector.scalar_tensor_tensor(kd, k3, sc_in, ta, ALU.mult, ALU.mult).then_inc(kd_ok, 1)
                dve.wait_ge(ebl_ok, i + 1)
                nc.vector.scalar_tensor_tensor(ke, k3, sc_in, tm, ALU.mult, ALU.mult).then_inc(ke_ok, 1)
                if first:
                    for k in range(KT):
                        dve.wait_ge(hi_o, k + 1)
                        nc.vector.scalar_tensor_tensor(wo[:, 1, k, :], woraw[:, k, :], g_out[:, k:k + 1],
                                                       wo[:, 0, k, :], ALU.mult, ALU.subtract).then_inc(lo_o, 1)
                if not first:
                    mixed_lo(i - 1)
                for w, (r, a, s) in enumerate(((0, 0, s2), (64, 0, s4), (0, 1, s2), (64, 1, s4))):
                    dve.wait_ge(w_sum, 4 * (i + 1))
                    dve.wait_ge(halo_ok, i + 2)
                    rr = slice(r, r + 64)
                    inv = 1.0 / (2, 4, 8, 16)[w]
                    if not first:
                        nc.vector.scalar_tensor_tensor(ub[rr, a, HALO:], s[rr, a, HALO:], inv, ub[rr, a, HALO:],
                                                       ALU.mult, ALU.subtract).then_inc(pooled, 1)
                    else:
                        nc.vector.tensor_tensor(s[rr, a, HALO:2 * HALO], s[rr, a, HALO:2 * HALO], cnt[rr, a, :],
                                                ALU.mult).then_inc(cut, 1)
                        nc.vector.scalar_tensor_tensor(ub[rr, a, 2 * HALO:], s[rr, a, 2 * HALO:], inv,
                                                       ub[rr, a, 2 * HALO:], ALU.mult, ALU.subtract)
                        dve.wait_ge(cut, w + 1)
                        nc.vector.tensor_tensor(ub[rr, a, HALO:2 * HALO], s[rr, a, HALO:2 * HALO],
                                                ub[rr, a, HALO:2 * HALO], ALU.subtract).then_inc(pooled, 1)
                mask = causal[:, :].bitcast(I32).unsqueeze(1).broadcast_to([P, 4, P])

                def masked(t):
                    if first:
                        dve.wait_ge(built, 3)
                        dve.wait_ge(cleared, 5)
                    dve.wait_ge(pe_sc, 2 * i + t + 1)
                    nc.vector.memset(idle[:, t:t + 1], 0.0)
                    nc.vector.copy_predicated(sT[:, t, :, :], mask, bank[6 + t][:, :].rearrange("p (a b) -> p a b", b=P)
                                              ).then_inc(sT_ok, 1)

                def mem_max(n):
                    dve.wait_ge(pe_ms, 4 * i + n + 1)
                    nc.vector.tensor_reduce(mx[:, 2 * n:2 * n + 2], bank[2 + n % 2][:, :].rearrange("p (h m) -> p h m", h=2),
                                            AX.X, ALU.max).then_inc(max_ok, 1)
                    dve.wait_ge(max_ok, 4 * i + n + 1)
                    nc.vector.tensor_scalar(nm[:, 2 * n:2 * n + 2], mx[:, 2 * n:2 * n + 2], -MSCALE, None,
                                            ALU.mult).then_inc(nmax_ok, 1)

                def p_norm(n):
                    dve.wait_ge(p_exp, 4 * i + n + 1)
                    nc.vector.reciprocal(rsum[:, 2 * n:2 * n + 2], psum_p[:, 2 * n:2 * n + 2]).then_inc(rs_ok, 1)
                    dve.wait_ge(rs_ok, 4 * i + n + 1)
                    r = rsum[:, 2 * n:2 * n + 2].unsqueeze(2).broadcast_to([P, 2, NMEM])
                    nc.vector.tensor_tensor(pr[n % 2], pr[n % 2], r, ALU.mult).then_inc(pn_ok, 1)

                def state(c, b):
                    dve.wait_ge(pe_st, 4 * i + c + 1)
                    if c == 0:
                        dve.wait_ge(s_carry, i + 1)
                        dve.wait_ge(dec_ok, i + 1)
                    else:
                        dve.wait_ge(s_ok, 4 * i + c)
                    for p in range(NPAIR):
                        for h in range(2):
                            r = slice(64 * h, 64 * h + 64)
                            a = nc.vector.scalar_tensor_tensor(
                                S[r, c + 1, p, :], S[r, c, p, :], dec[r, p, c:c + 1],
                                bank[b][r, p * 256 + h * P:p * 256 + (h + 1) * P], ALU.mult, ALU.add)
                    a.then_inc(s_ok, 1)

                def pt_copy(n, b):
                    t, p = n // NPAIR, n % NPAIR
                    dve.wait_ge(pe_pt, 4 * i + n + 1)
                    dve.wait_ge(pe_p2, 6 * (i + 1))
                    nc.vector.tensor_copy(pt[:, p, :, t * P:(t + 1) * P],
                                          b16[b].rearrange("p (a b) -> p a b", b=P)).then_inc(pt_out, 1)

                def head(p, b):
                    dve.wait_ge(o_r, 2 * i + p + 1)
                    nc.vector.tensor_tensor(osq[p], osq[p], gate[:, 2 * p:2 * p + 2, :], ALU.mult).then_inc(og_ok, 1)
                    dve.wait_ge(og_ok, 2 * i + p + 1)
                    nc.vector.tensor_tensor(mixed[:, 2 * p:2 * p + 2, :], bank[b][:, :].rearrange("p (a t) -> p a t", a=2),
                                            osq[p], ALU.mult).then_inc(mix_g, 1)

                def rows(n):
                    if not first:
                        add_rows(i - 1, n)

                masked(0)
                masked(1)
                mem_max(0)
                mem_max(1)
                p_norm(0)
                p_norm(1)
                rows(0)
                state(0, 5)
                state(1, 4)
                mem_max(2)
                mem_max(3)
                pt_copy(0, 6)
                p_norm(2)
                p_norm(3)
                rows(1)
                state(2, 5)
                pt_copy(1, 7)
                state(3, 4)
                pt_copy(2, 6)
                if not first:
                    norm_rows(i - 1, 0)
                pt_copy(3, 7)
                if not last:
                    normalise(i + 1)
                    dve.wait_ge(xn_ok, i + 2)
                rows(2)
                dve.wait_ge(p2_out, 6 * i + 5)
                dve.wait_ge(pooled, 4 * (i + 1))
                nc.vector.tensor_tensor(mixed[:, 4:6, :], ub[:, :, HALO:], gate[:, 4:6, :], ALU.mult).then_inc(mix_p, 1)
                dve.wait_ge(pe_pv, i + 1)
                nc.vector.scalar_tensor_tensor(mixed[:, 6:8, :], bank[2][:, :].rearrange("p (a t) -> p a t", a=2), i_v,
                                               gate[:, 6:8, :], ALU.mult, ALU.mult).then_inc(mix_m, 1)
                rows(3)
                head(0, 5)
                head(1, 4)
                dve.wait_ge(mix_p, i + 1)
                dve.wait_ge(mix_m, i + 1)
                dve.wait_ge(mix_g, 2 * (i + 1))
                nc.vector.tensor_reduce(mmax[:, 1:2], mixed, AX.XY, ALU.max,
                                        apply_absolute_value=True).then_inc(mmax_ok, 1)
                if not first:
                    norm_rows(i - 1, 1)

            def tail(n):
                mixed_lo(n - 1)
                for t in range(NT):
                    add_rows(n - 1, 2 * t)
                    add_rows(n - 1, 2 * t + 1)
                    norm_rows(n - 1, t)

            m_tiny, m_exp, m_inv, sc_ok, cut = (sem(n) for n in ("m_tiny", "m_exp", "m_inv", "sc_ok", "cut"))
            run_blocks(dve, step, tail)

        @block.gpsimd
        def _(pool):
            nc.gpsimd.memset(ones[:, :], 1.0).then_inc(built, 1)
            nc.gpsimd.memset(eps[:, 0:1], EPS)
            nc.gpsimd.memset(eps[:, 1:2], float(np.log(2.0 ** XBITS)))
            nc.gpsimd.memset(ident[:, :], 0.0).then_inc(ident_ok, 1)
            nc.gpsimd.memset(causal[:, :], 1.0).then_inc(ident_ok, 1)
            pool.wait_ge(ident_ok, 2)
            nc.gpsimd.affine_select(out=ident[:, :], in_=ident[:, :], compare_op=ALU.not_equal, fill=1.0, base=0,
                                    pattern=[[-1, P]], channel_multiplier=1).then_inc(ident_ok, 1)
            nc.gpsimd.affine_select(out=causal[:, :], in_=causal[:, :], compare_op=ALU.is_ge, fill=0.0, base=0,
                                    pattern=[[1, P]], channel_multiplier=-1).then_inc(ident_ok, 1)
            pool.wait_ge(ident_ok, 4)
            nc.gpsimd.memset(causal[0:64, 64:128], 0.0).then_inc(built, 1)
            nc.gpsimd.tensor_copy(ident16[:, :], ident[:, :]).then_inc(built, 1)

            def fold_rows(buf, n0, signal):
                for n, half in enumerate((4, 2, 1)):
                    if n:
                        pool.wait_ge(signal, n0 + n)
                    nc.gpsimd.tensor_tensor(buf[:, 0:half, :], buf[:, 0:half, :], buf[:, half:2 * half, :],
                                            ALU.add).then_inc(signal, 1)

            def x_lo_of(n):
                for h in range(2):
                    k = slice(h * KT // 2, (h + 1) * KT // 2)
                    pool.wait_ge(x_hi, 2 * n + h + 1)
                    nc.gpsimd.tensor_tensor(xn[:, 1, k, :], xb[:, k, :], xn[:, 0, k, :],
                                            ALU.subtract).then_inc(x_lo, 1)

            pool.wait_ge(mem_sq, 1)
            fold_rows(msq, 0, mem_sum)
            for n in range(3):
                pool.wait_ge(mmax_ok, n + 1)
                nc.gpsimd.partition_all_reduce(mmax[:, 2:3], mmax[:, 1:2], P, RMAX).then_inc(max_all, 1)
                if n == 1:
                    pool.wait_ge(scaled, 2)
                    lr = wraw[:, :, CLR:DIN]
                    nc.gpsimd.tensor_tensor(lr, lr, gs.unsqueeze(2).broadcast_to([P, KT, RANK]),
                                            ALU.mult).then_inc(low_rank, 1)
                    pool.wait_ge(low_rank, 1)
                    nc.gpsimd.tensor_copy(wlr[:, :, 0:RANK], lr).then_inc(low_rank, 1)
                    pool.wait_ge(low_rank, 2)
                    nc.gpsimd.tensor_tensor(wlr[:, :, RANK:], lr, wlr[:, :, 0:RANK], ALU.subtract).then_inc(low_rank, 1)
                    pool.wait_ge(x_sq, 1)
                    fold_rows(sq, 0, sq_add)
                    x_lo_of(0)
            wait_split(pool, KT - 1)
            nc.gpsimd.memset(ub[:, :, 0:HALO], 0.0).then_inc(halo_ok, 1)
            nc.gpsimd.memset(qb, 0.0).then_inc(cleared, 1)
            pool.wait_ge(hi_o, KT)
            pool.wait_ge(lo_o, KT)
            nc.gpsimd.memset(kab, 0.0).then_inc(cleared, 1)
            nc.gpsimd.memset(sT, 0.0).then_inc(cleared, 1)
            nc.gpsimd.memset(S[:, 0, :, :], 0.0).then_inc(s_carry, 1)

            def p_lo_of(i, n):
                pool.wait_ge(p_hi, 4 * i + n + 1)
                nc.gpsimd.tensor_tensor(phl[n % 2][:, 1, :, :], pr[n % 2], phl[n % 2][:, 0, :, :],
                                        ALU.subtract).then_inc(p_lo, 1)

            def step(i, first, last):
                L = HALO + TB
                pool.wait_ge(p2_out, 6 * i + 3)
                pool.wait_ge(ke_ok, i + 1)
                pool.wait_ge(q_ok, 2 * (i + 1))
                nc.gpsimd.tensor_tensor(s2[:, :, 1:L], ub[:, :, 1:L], ub[:, :, 0:L - 1], ALU.add).then_inc(w_sum, 1)
                pool.wait_ge(w_sum, 4 * i + 1)
                nc.gpsimd.tensor_tensor(s4[:, :, 3:L], s2[:, :, 3:L], s2[:, :, 1:L - 2], ALU.add).then_inc(w_sum, 1)
                nc.gpsimd.tensor_copy(ub[:, :, 0:HALO], ub[:, :, TB:TB + HALO]).then_inc(halo_ok, 1)
                pool.wait_ge(w_sum, 4 * i + 2)
                nc.gpsimd.tensor_tensor(s2[:, 1, 7:L], s4[:, 1, 7:L], s4[:, 1, 3:L - 4], ALU.add).then_inc(w_sum, 1)
                pool.wait_ge(w_sum, 4 * i + 3)
                nc.gpsimd.tensor_tensor(s4[:, 1, 15:L], s2[:, 1, 15:L], s2[:, 1, 7:L - 8], ALU.add).then_inc(w_sum, 1)
                if not last:
                    pool.wait_ge(x_sq, i + 2)
                    fold_rows(sq, 3 * (i + 1), sq_add)
                for n in range(4):
                    p_lo_of(i, n)
                if not last:
                    x_lo_of(i + 1)
                if not first:
                    pool.wait_ge(m_sc, i)
                pool.wait_ge(mmax_ok, i + 4)
                nc.gpsimd.tensor_tensor(idle[:, 2:3], eps[:, 0:1], eps[:, 1:2], ALU.add)
                nc.gpsimd.tensor_copy(S[:, 0, :, :], S[:, NC, :, :]).then_inc(s_carry, 1)
                nc.gpsimd.partition_all_reduce(mmax[:, 2:3], mmax[:, 1:2], P, RMAX).then_inc(m_all, 1)

            run_blocks(pool, step, lambda n: None)


def kernel(**inputs):
    import concourse.bacc as bacc
    from concourse.bass_utils import run_bass_kernel_spmd

    a = {k: np.asarray(v) for k, v in inputs.items()}
    T = a["x"].shape[1]

    def tiled(w):
        return np.ascontiguousarray(w.reshape(-1, P, w.shape[1]).transpose(1, 0, 2))

    def column(g):
        return g.reshape(-1, P).T

    w = a["w_in"]
    sizes = (256, 256, 512, RANK, 512, 256, 256, 256, 256)
    q, k, v, lr, gg, u, gp, qm, gm = np.split(w, np.cumsum(sizes)[:-1], axis=1)
    counts = np.zeros((P, 2, HALO), np.float32)
    for g, win in enumerate((2, 4, 8, 16)):
        counts[64 * (g % 2):64 * (g % 2) + 64, g // 2] = 1.0 / np.minimum(np.arange(HALO) + 1, win)
    unit = np.ones((P, 2), np.float32)
    arrays = {
        "xt": np.ascontiguousarray(a["x"][0].T.reshape(KT, P, T // TB, TB).transpose(2, 1, 0, 3)),
        "x": np.ascontiguousarray(a["x"][0]),
        "memt": tiled(np.ascontiguousarray(a["mem"][0].T)),
        "w_in": tiled(np.concatenate([q, k, v, gg, gp, gm, qm, lr], axis=1)),
        "w_ut": tiled(np.ascontiguousarray(u.T)),
        "w_gk_up": np.ascontiguousarray(a["w_gk_up"]),
        "vecs": np.ascontiguousarray(np.concatenate(
            [column(a["norm_g"]), column(a["mem_norm_g"]), column(a["b_gk"])]
            + [column(a["gla_norm_g"])] * HEADS + [column(a["pool_scale"]), unit], axis=1)),
        "pool_w": np.ascontiguousarray(a["pool_w"]),
        "counts": counts,
        "w_mem": tiled(a["w_mem_kv"]),
        "w_out": tiled(a["w_out"]),
        "final_g": np.ascontiguousarray(a["final_g"]),
    }
    nc = bacc.Bacc("TRN2", target_bir_lowering=False, num_devices=1)
    args = [nc.dram_tensor(f"in_{n}", x.shape, mybir.dt.from_np(x.dtype), kind="ExternalInput").ap()
            for n, x in arrays.items()]
    out = nc.dram_tensor("out", (T, D), F32, kind="ExternalOutput").ap()
    hybrid_block(nc, *args, out)
    r = run_bass_kernel_spmd(nc, [{f"in_{n}": x for n, x in arrays.items()}], core_ids=[0])
    return r.results[0]["out"].reshape(a["x"].shape)
```

```python
from contextlib import ExitStack

import numpy as np

import concourse.bass as bass
from concourse import mybir

ALU = mybir.AluOpType
ACT = mybir.ActivationFunctionType
AX = mybir.AxisListType
F32 = mybir.dt.float32
F16 = mybir.dt.float16
I32 = mybir.dt.int32
BF16 = mybir.dt.bfloat16
RMAX = bass.bass_isa.ReduceOp.absmax

P = 128
D = 1024
KT = D // P
TB = 256
NT = TB // P
CHUNK = 64
NC = TB // CHUNK
HEADS = 4
DK = 64
DV = 128
RANK = 16
NPAIR = HEADS // 2
NMEM = 256
MT = NMEM // P
HALO = 16
EPS = 1e-6
NORMALIZER = 16.0
QSCALE = DK ** -0.5
MSCALE = 64 ** -0.5

CQ, CK, CV, CG, CU, CGP, CGM, CQM, CLR = 0, 256, 512, 1024, 1536, 1792, 2048, 2304, 2560
DIN = CLR + RANK
WIDE = CLR

TOP = 14
EXP_MASK = 0x7F800000
SCALE_FIELD = float((127 + TOP + 127) << 23)
INV_FIELD = float(-(TOP << 23))
TINY = 2.0 ** -100
XBITS = 10
QBITS = 5 + XBITS + 5 + TOP + 1 - 15

MEM_AFTER = 5
EXP_LN = "natural_log_exp_and_others"

O_X, O_XN, O_MIX, O_T, O_U, O_QB = 0, 8192, 16384, 24576, 33024, 35200
O_KD, O_KE, O_V, O_WO, O_GATE = 39296, 41344, 43392, 47488, 80256
O_MHL, O_KAB, O_ST, O_S, O_Y, O_QM, O_END = 88448, 96640, 100736, 104832, 109952, 114048, 116096
O_TAIL = DIN * KT * 4


def hybrid_block(nc, xt, x, memt, w_in, w_ut, w_gk_up, vecs, pool_w, counts, w_mem, w_out, final_g, out):
    NB = xt.shape[0]
    ctx = ExitStack()
    with ctx:
        def sb(name, shape, dt):
            return ctx.enter_context(nc.sbuf_tensor(name, shape, dt))

        def sem(name):
            return ctx.enter_context(nc.semaphore(name))

        whl = sb("whl", [P, 2, KT, WIDE], F16)
        wlr = sb("wlr", [P, KT, 2 * RANK], F16)
        arena = sb("arena", [P, O_END // 4], F32)
        ident = sb("ident", [P, P], F32)
        ident16 = sb("ident16", [P, P], F16)
        ones = sb("ones", [P, P], F32)
        causal = sb("causal", [P, P], F32)
        keep = sb("keep", [P, TB], BF16)
        fg = sb("fg", [P, D], F32)
        kst = sb("kst", [P, NPAIR, 2, 2, NMEM], F16)
        vm = sb("vm", [P, 2, MT, 256], F16)
        up2 = sb("up2", [2 * RANK, 256], F32)
        cnt = sb("cnt", [P, 2, HALO], F32)
        vec = sb("vec", [P, 32], F32)
        eps = sb("eps", [P, 2], F32)
        sca = sb("sca", [P, 34], F32)
        dec = sb("dec", [P, NPAIR, NC], F32)
        mx = sb("mx", [P, 8], F32)
        nm = sb("nm", [P, 8], F32)
        psum_p = sb("psum_p", [P, 8], F32)
        rsum = sb("rsum", [P, 8], F32)
        wmx = sb("wmx", [P, 2, KT], F32)
        small = sb("small", [P, 16], F32)
        ysum, yr, mmax = small[:, 0:2], small[:, 2:4], small[:, 4:8]
        kvmax = small[:, 8:12]
        idle = small[:, 12:15]

        g_in, g_mem, b_gk, g_out = vec[:, 0:8], vec[:, 8:16], vec[:, 16:18], vec[:, 18:26]

        def view(off, shape, dt):
            size = int(np.prod(shape)) * (2 if dt in (F16, BF16) else 4)
            ap = arena[:, off // 4:(off + size) // 4]
            if dt != F32:
                ap = ap.bitcast(dt)
            if len(shape) == 2:
                ap = ap.rearrange("p (a b) -> p a b", b=shape[1])
            if len(shape) == 3:
                ap = ap.rearrange("p (a b c) -> p a b c", b=shape[1], c=shape[2])
            if len(shape) == 4:
                ap = ap.rearrange("p (a b c d) -> p a b c d", b=shape[1], c=shape[2], d=shape[3])
            return ap

        xb = view(O_X, [KT, TB], F32)
        xn = view(O_XN, [2, KT, TB], F16)
        mixed = view(O_MIX, [KT, TB], F32)
        sq = view(O_MIX, [KT, TB], F32)
        ta = view(O_T, [2, TB], F32)
        tm = view(O_T + 2048, [2, TB], F32)
        tb = view(O_T + 4096, [2, TB], F32)
        te = view(O_T + 6144, [2, TB], F32)
        lrs = view(O_KE, [TB], F32)
        s2 = view(O_T, [2, HALO + TB], F32)
        s4 = view(O_T + 2176, [2, HALO + TB], F32)
        junk = view(O_QM, [D], BF16)
        pr = [view(O_T + 2048 * b, [2, NMEM], F32) for b in range(2)]
        phl = [view(O_T + 4096 + 2048 * b, [2, 2, NMEM], F16) for b in range(2)]
        ub = view(O_U, [2, HALO + TB], F32)
        qb = view(O_QB, [NPAIR, 2, TB], F32)
        kd = view(O_KD, [NPAIR, TB], F32)
        ke = view(O_KE, [NPAIR, TB], F32)
        osq = [view(o, [2, TB], F32) for o in (O_KD, O_KE)]
        v = view(O_V, [NT, 512], F32)
        wo = view(O_WO, [2, KT, D], F16)
        gate = view(O_GATE, [KT, TB], F32)
        mhl = view(O_MHL, [2, KT, TB], F16)
        pt = view(O_XN, [NPAIR, 8, TB], F16)
        kab = view(O_KAB, [NT * HEADS, 2, 64], F32)
        sT = view(O_ST, [NT, 2 * NPAIR, P], F32)
        S = view(O_S, [NC + 1, NPAIR, P], F32)
        yb = view(O_Y, [D], F32)
        qst = view(O_QM, [NPAIR, 2, TB], F16)
        wraw = view(0, [KT, DIN], F32)
        woraw = view(O_TAIL, [KT, D], F32)
        xb0 = view(O_TAIL, [KT, TB], F32)
        sq0 = view(O_TAIL + 8192, [KT, TB], F32)
        memb = view(O_TAIL, [KT, NMEM], F32)
        wmraw = view(O_TAIL + 8192, [KT, 512], F32)
        wflat = whl[:, :, :, :].rearrange("p a b c -> p (a b c)").bitcast(F32)
        wut = wflat[:, 0:2048].rearrange("p (a b) -> p a b", a=2)
        pwb = wflat[:, 2048:2304].rearrange("p (a b) -> p a b", a=2)
        msq = wflat[:, 2304:2304 + KT * NMEM].rearrange("p (a b) -> p a b", a=KT)
        rmem = wflat[:, 4608:4608 + NMEM]

        bank = [ctx.enter_context(nc.psum_tensor(f"bank{i}", [P, 512], F32)) for i in range(8)]
        kraw = bank[1][:, :].rearrange("p (a b) -> p a b", a=NPAIR)
        vraw = bank[2][:, :].rearrange("p (a b) -> p a b", a=MT)
        b16 = {i: bank[i][:, :].bitcast(F16) for i in (6, 7)}

        def col(n):
            return sca[:, n:n + 1]
        s_w, i_w, s_o, i_o, s_m, i_m, sc_in, sc_q, sc_out = (col(n) for n in range(9))
        s_vk, i_vk, e_vk, m_vk = (sca[:, n:n + 2] for n in (22, 24, 26, 28))
        s_v, s_k, i_v, i_k = (col(n) for n in (22, 23, 24, 25))
        sc_ms, sc_neg = col(30), col(31)
        gs = sca[:, 12:20]
        e_tmp = col(20)
        m_tmp = col(21)

        d_vec, d_mem, d_wut, d_wout, d_x, d_res, d_store = (
            sem(n) for n in ("d_vec", "d_mem", "d_wut", "d_wout", "d_x", "d_res", "d_store"))
        d_w = [sem(f"d_w{k}") for k in range(KT)]
        cleared, built, ident_ok, mem_sq, mem_sum, mem_ms, mem_ln, mem_r, mem_n = (
            sem(n) for n in ("cleared", "built", "ident_ok", "mem_sq", "mem_sum", "mem_ms", "mem_ln", "mem_r", "mem_n"))
        memk_done, memv_done, fold_done, fold_out = (
            sem(n) for n in ("memk_done", "memv_done", "fold_done", "fold_out"))
        max_in, max_all, hi_w, lo_w, hi_v, lo_v, hi_k, lo_k, hi_o, lo_o, scaled = (
            sem(n) for n in ("max_in", "max_all", "hi_w", "lo_w", "hi_v", "lo_v", "hi_k", "lo_k", "hi_o", "lo_o",
                             "scaled"))
        low_rank, qm_hi, qm_lo = (sem(n) for n in ("low_rank", "qm_hi", "qm_lo"))
        pe_lr, pe_q, pe_k, pe_logit, pe_v, pe_p2, pe_out, pe_ket, pe_sc, pe_ms, pe_st, pe_rb, pe_pt, pe_o, pe_msq, pe_pv = (
            sem(n) for n in ("pe_lr", "pe_q", "pe_k", "pe_logit", "pe_v", "pe_p2", "pe_out", "pe_ket", "pe_sc",
                             "pe_ms", "pe_st", "pe_rb", "pe_pt", "pe_o", "pe_msq", "pe_pv"))
        lr_out, abs_ok, expabs, softplus, eb_ok, enb_ok, ebl_ok, v_out, p2_out, y_sq, y_ln, y_r, x_sq = (
            sem(n) for n in ("lr_out", "abs_ok", "expabs", "softplus", "eb_ok", "enb_ok", "ebl_ok", "v_out",
                             "p2_out", "y_sq", "y_ln", "y_r", "x_sq"))
        ket_out, p_exp, p_hi, rb_ln, rb_ok, x_hi, o_sq, o_ln, o_r, m_hi = (
            sem(n) for n in ("ket_out", "p_exp", "p_hi", "rb_ln", "rb_ok", "x_hi", "o_sq", "o_ln", "o_r", "m_hi"))
        z_ok, gk_ok, b_ok, bl_ok, q_ok, dec_ok, kd_ok, ke_ok, pooled, y_add, y_ok = (
            sem(n) for n in ("z_ok", "gk_ok", "b_ok", "bl_ok", "q_ok", "dec_ok", "kd_ok", "ke_ok", "pooled",
                             "y_add", "y_ok"))
        sT_ok, max_ok, nmax_ok, rs_ok, pn_ok, s_ok, pt_out, xn_ok, og_ok, mix_g, mix_m, mix_p, mmax_ok, m_sc, m_lo = (
            sem(n) for n in ("sT_ok", "max_ok", "nmax_ok", "rs_ok", "pn_ok", "s_ok", "pt_out", "xn_ok", "og_ok",
                             "mix_g", "mix_m", "mix_p", "mmax_ok", "m_sc", "m_lo"))
        w_sum, halo_ok, sq_add, p_lo, x_lo, m_all, s_carry = (
            sem(n) for n in ("w_sum", "halo_ok", "sq_add", "p_lo", "x_lo", "m_all", "s_carry"))

        block = ctx.enter_context(nc.Block())

        def wait_split(eng, k):
            eng.wait_ge(hi_w, k + 1)
            eng.wait_ge(lo_w, k + 1)

        def run_blocks(eng, step, tail):
            step(0, True, False)
            with eng.Fori(1, NB - 1) as i:
                step(i, False, False)
            step(NB - 1, False, True)
            tail(NB)

        @block.sync
        def _(sp):
            sp.dma_start(vec[:, 0:26], vecs).then_inc(d_vec, 16)
            sp.dma_start(cnt[:, :, :], counts).then_inc(d_vec, 16)
            sp.dma_start(up2[0:RANK, :], w_gk_up).then_inc(d_vec, 16)
            sp.dma_start(up2[RANK:2 * RANK, :], w_gk_up).then_inc(d_vec, 16)
            sp.dma_start(fg[:, :], final_g.partition_broadcast(P)).then_inc(d_vec, 16)
            sp.dma_start(memb, memt).then_inc(d_mem, 16)
            sp.dma_start(wmraw, w_mem).then_inc(d_mem, 16)
            sp.dma_start(wut, w_ut).then_inc(d_wut, 16)
            sp.wait_ge(cleared, 1)
            for g in range(4):
                h = g % 2
                sp.dma_start(pwb[64 * h:64 * h + 64, g // 2, 64 * h:64 * h + 64], pool_w[g]).then_inc(d_wut, 16)
            for k in range(KT):
                sp.dma_start(wraw[:, k, 0:CU], w_in[:, k, 0:CU]).then_inc(d_w[k], 16)
                sp.dma_start(wraw[:, k, CGP:DIN], w_in[:, k, CU:DIN - 256]).then_inc(d_w[k], 16)
            sp.wait_ge(memk_done, 1)
            sp.wait_ge(memv_done, 1)
            sp.dma_start(xb0, xt[0]).then_inc(d_x, 16)
            sp.wait_ge(x_hi, 2)
            sp.wait_ge(x_lo, 2)
            sp.dma_start(woraw, w_out).then_inc(d_wout, 16)

            def outputs(j, t):
                rows = bass.ds(j * TB + t * P, P)
                if isinstance(j, int) and j == 0 and t == 0:
                    sp.wait_ge(lo_o, KT)
                    sp.wait_ge(hi_o, KT)
                else:
                    sp.wait_ge(d_store, (j * NT + t) * 16)
                sp.dma_start(yb, x[rows, :]).then_inc(d_res, 16)
                sp.wait_ge(y_ok, j * NT + t + 1)
                sp.dma_start(out[rows, :], yb).then_inc(d_store, 16)

            def step(i, first, last):
                if not last:
                    sp.wait_ge(x_hi, 2 * (i + 1))
                    sp.wait_ge(x_lo, 2 * (i + 1))
                    if first:
                        wait_split(sp, 0)
                    sp.dma_start(xb, xt[i + 1] if first else xt[bass.ds(i + 1, 1)].rearrange(
                        "a p k t -> (a p) k t")).then_inc(d_x, 16)
                if not first:
                    for t in range(NT):
                        outputs(i - 1, t)

            def tail(n):
                for t in range(NT):
                    outputs(n - 1, t)
                sp.wait_ge(d_store, 16 * NT * n)

            run_blocks(sp, step, tail)

        @block.tensor
        def _(pe):
            pe.wait_ge(d_wut, 16 * 5)
            for k in range(KT):
                for g in range(2):
                    mm = nc.tensor.matmul(bank[4 + k // 2][:, (k % 2) * 256 + g * P:(k % 2) * 256 + g * P + P],
                                          wut[:, g, k * P:(k + 1) * P], pwb[:, g, :], start=True, stop=True)
            mm.then_inc(fold_done, 1)
            pe.wait_ge(built, 3)
            pe.wait_ge(mem_sum, 3)
            nc.tensor.matmul(bank[0][:, 0:NMEM], ones[:, :], msq[:, 0, :], start=True, stop=True).then_inc(mem_ms, 1)
            pe.wait_ge(mem_n, KT)
            for j in range(2):
                for k in range(KT):
                    mm = nc.tensor.matmul(bank[1][:, j * NMEM:(j + 1) * NMEM], wmraw[:, k, j * P:(j + 1) * P],
                                          memb[:, k, :], start=k == 0, stop=k == KT - 1)
            mm.then_inc(memk_done, 1)
            for j in range(MT):
                for k in range(KT):
                    mm = nc.tensor.matmul(bank[2][:, j * 256:(j + 1) * 256], memb[:, k, j * P:(j + 1) * P],
                                          wmraw[:, k, 256:512], start=k == 0, stop=k == KT - 1)
            mm.then_inc(memv_done, 1)

            def rms_sum(n):
                pe.wait_ge(sq_add, 3 * (n + 1))
                squared = sq0 if isinstance(n, int) and n == 0 else sq
                nc.tensor.matmul(bank[3][:, 0:TB], ones[:, :], squared[:, 0, :], start=True, stop=True).then_inc(pe_rb, 1)

            rms_sum(0)

            def split(ap, tiles, parts):
                last = (tiles - 1, 2)
                for k in range(tiles):
                    for n, (a, b) in enumerate(((0, 0), (0, 1), (1, 0))):
                        lhs, rhs = parts(k, a, b)
                        mm = nc.tensor.matmul(ap, lhs, rhs, start=k == 0 and n == 0, stop=(k, n) == last)
                return mm

            def features(b, c0, arriving=False):
                def parts(k, p, r, c):
                    if arriving:
                        wait_split(pe, k)
                    return whl[:, p, k, c:c + P], xn[:, r, k, :]

                for j in range(2):
                    mm = split(bank[b][:, j * TB:(j + 1) * TB], KT,
                               lambda k, p, r, c=c0 + j * P: parts(k, p, r, c))
                return mm

            def out_proj(j, n):
                t, h = n // 2, n % 2
                if n == 0:
                    pe.wait_ge(m_hi, j + 1)
                    pe.wait_ge(m_lo, j + 1)
                if n >= 2:
                    pe.wait_ge(y_add, 4 * j + n + 3)
                split(bank[h][:, :], KT, lambda k, p, r: (mhl[:, p, k, t * P:(t + 1) * P],
                                                          wo[:, r, k, h * 512:(h + 1) * 512])).then_inc(pe_out, 1)

            def bank_free(i, first, b):
                if first:
                    return
                pe.wait_ge(y_add, 4 * i - 1 + b)

            def step(i, first, last):
                if first:
                    pe.wait_ge(low_rank, 3)
                    pe.wait_ge(lo_v, 1)
                    pe.wait_ge(lo_k, 4)
                pe.wait_ge(x_hi, 2 * (i + 1))
                pe.wait_ge(x_lo, 2 * (i + 1))
                bank_free(i, first, 0)
                for r in range(2):
                    for k in range(KT):
                        mm = nc.tensor.matmul(bank[0][0:2 * RANK, 0:TB], wlr[:, k, :], xn[:, r, k, :],
                                              start=r == 0 and k == 0, stop=r == 1 and k == KT - 1)
                mm.then_inc(pe_lr, 1)
                bank_free(i, first, 1)
                features(1, CQ, arriving=first).then_inc(pe_q, 1)
                pe.wait_ge(rb_ok, i + 1)
                pe.wait_ge(lr_out, i + 1)
                for j in range(2):
                    mm = nc.tensor.matmul(bank[3][:, j * TB:(j + 1) * TB], up2[:, j * P:(j + 1) * P],
                                          lrs[0:2 * RANK, :], start=True, stop=True)
                mm.then_inc(pe_logit, 1)
                if not first:
                    pe.wait_ge(mix_m, i)
                features(2, CK).then_inc(pe_k, 1)
                for t in range(NT):
                    if t == 1:
                        pe.wait_ge(q_ok, 2 * (i + 1))
                    split(bank[t][:, :], KT, lambda k, p, r: (xn[:, p, k, t * P:(t + 1) * P],
                                                               whl[:, r, k, CV:CV + 512])).then_inc(pe_v, 1)
                pe.wait_ge(ke_ok, i + 1)
                features(2, CG).then_inc(pe_p2, 1)
                pe.wait_ge(z_ok, 2 * (i + 1))
                features(3, CG + 256).then_inc(pe_p2, 1)
                for n, c in enumerate((CU, CGP, CGM, CQM)):
                    if n < 2:
                        pe.wait_ge(v_out, 2 * i + n + 1)
                    else:
                        pe.wait_ge(p2_out, 5 * i + n - 1)
                    features(n, c).then_inc(pe_p2, 1)
                pe.wait_ge(ke_ok, i + 1)
                if not first:
                    pe.wait_ge(mix_g, 2 * i)
                else:
                    pe.wait_ge(fold_out, 4)
                for t in range(NT):
                    for p in range(NPAIR):
                        n = t * NPAIR + p
                        mm = nc.tensor.transpose(bank[4][:, n * P:(n + 1) * P], ke[:, p, t * P:(t + 1) * P],
                                                 ident[:, :])
                mm.then_inc(pe_ket, 1)
                pe.wait_ge(kd_ok, i + 1)
                pe.wait_ge(q_ok, 2 * (i + 1))
                for t in range(NT):
                    if not first:
                        pe.wait_ge(pt_out, 4 * i - 1 + t)
                    for p in range(NPAIR):
                        mm = nc.tensor.matmul(bank[6 + t][:, p * 256:(p + 1) * 256], kd[:, p, t * P:(t + 1) * P],
                                              qb[:, p, :, t * P:(t + 1) * P], start=True, stop=True)
                    mm.then_inc(pe_sc, 1)

                def mem_scores(n):
                    t, p, b = n // NPAIR, n % NPAIR, 2 + n % 2
                    if n < 2:
                        pe.wait_ge(p2_out, 5 * (i + 1))
                        pe.wait_ge(qm_lo, 2 * (i + 1))
                    else:
                        pe.wait_ge(p_exp, 4 * i + n - 1)
                    for h in range(2):
                        for r in range(2):
                            mm = nc.tensor.matmul(bank[b][:, h * NMEM:(h + 1) * NMEM], qst[:, p, h, t * P:(t + 1) * P],
                                                  kst[:, p, h, r, :], start=r == 0, stop=r == 1)
                    mm.then_inc(pe_ms, 1)

                def states(t, b):
                    for h in range(HEADS):
                        mm = nc.tensor.matmul(bank[b][:, h * DV:(h + 1) * DV], kab[:, t * HEADS + h, :, :],
                                              v[:, t, h * DV:(h + 1) * DV], start=True, stop=True)
                    mm.then_inc(pe_st, 1)

                def turn_p(n, b):
                    pe.wait_ge(p_hi, 4 * i + n + 1)
                    pe.wait_ge(p_lo, 4 * i + n + 1)
                    for h in range(2):
                        for m in range(MT):
                            for r in range(2):
                                j = (h * MT + m) * 2 + r
                                mm = nc.tensor.transpose(b16[b][:, j * P:(j + 1) * P],
                                                         phl[n % 2][:, r, h, m * P:(m + 1) * P], ident16[:, :])
                    mm.then_inc(pe_pt, 1)

                def head_out(p, b):
                    for t in range(NT):
                        for h in range(2):
                            nc.tensor.matmul(bank[b][:, h * TB + t * P:h * TB + (t + 1) * P],
                                             v[:, t, (2 * p + h) * DV:(2 * p + h + 1) * DV],
                                             sT[:, t, 2 * p + h, :], start=t == 0 and h == 0, stop=False,
                                             skip_group_check=True)
                    o3 = bank[b][:, :].rearrange("p (h t) -> p h t", h=2)
                    for c in range(NC):
                        mm = nc.tensor.matmul(o3[:, :, c * CHUNK:(c + 1) * CHUNK], S[:, c, p, :],
                                              qb[:, p, :, c * CHUNK:(c + 1) * CHUNK], start=False,
                                              stop=c == NC - 1, skip_group_check=True)
                    mm.then_inc(pe_o, 1)

                def head_ms(p):
                    pe.wait_ge(o_sq, 2 * i + p + 1)
                    nc.tensor.matmul(bank[6 + p][:, :], ones[:, :], osq[p], start=True,
                                     stop=True).then_inc(pe_msq, 1)

                def quarter(n):
                    if not first:
                        if n < 2:
                            pe.wait_ge(p2_out, 5 * i + 3 + n)
                        out_proj(i - 1, n)

                mem_scores(0)
                mem_scores(1)
                quarter(0)
                pe.wait_ge(ket_out, 2 * (i + 1))
                pe.wait_ge(v_out, 2 * (i + 1))
                states(0, 5)
                states(1, 4)
                mem_scores(2)
                mem_scores(3)
                pe.wait_ge(sT_ok, 2 * i + 1)
                turn_p(0, 6)
                quarter(1)
                pe.wait_ge(sT_ok, 2 * i + 2)
                turn_p(1, 7)
                pe.wait_ge(pt_out, 4 * i + 1)
                turn_p(2, 6)
                quarter(2)
                if not last:
                    pe.wait_ge(p_exp, 4 * i + 4)
                    rms_sum(i + 1)
                pe.wait_ge(pt_out, 4 * i + 2)
                turn_p(3, 7)
                pe.wait_ge(s_ok, 4 * i + 3)
                head_out(0, 5)
                pe.wait_ge(s_ok, 4 * i + 4)
                head_out(1, 4)
                pe.wait_ge(pt_out, 4 * i + 4)
                pe.wait_ge(p_exp, 4 * i + 3)
                for p in range(NPAIR):
                    for m in range(MT):
                        for n, (a, b) in enumerate(((0, 0), (0, 1), (1, 0))):
                            for h in range(2):
                                c = (2 * p + h) * 64
                                mm = nc.tensor.matmul(bank[2][64 * h:64 * h + 64, p * TB:(p + 1) * TB],
                                                      vm[:, a, m, c:c + 64], pt[:, p, (h * MT + m) * 2 + b, :],
                                                      start=m == 0 and n == 0, stop=m == MT - 1 and n == 2)
                mm.then_inc(pe_pv, 1)
                if last:
                    head_ms(0)
                    head_ms(1)
                    quarter(3)
                else:
                    quarter(3)
                    head_ms(0)
                    head_ms(1)

            def tail(n):
                for b in range(4):
                    if b < 2:
                        bank_free(n, False, b)
                    out_proj(n - 1, b)

            run_blocks(pe, step, tail)

        @block.scalar
        def _(act):
            nc.scalar.preload_act_table_set(EXP_LN)
            act.wait_ge(d_mem, 32)
            nc.scalar.activation(msq, memb, ACT.Square).then_inc(mem_sq, 1)
            act.wait_ge(fold_done, 1)
            for n in range(4):
                nc.scalar.activation(wraw[:, 2 * n:2 * n + 2, CU:CU + 256],
                                     bank[4 + n][:, :].rearrange("p (a b) -> p a b", a=2), ACT.Copy).then_inc(fold_out, 1)
            act.wait_ge(mem_ms, 1)
            act.wait_ge(built, 3)
            nc.scalar.activation(rmem, bank[0][:, 0:NMEM], ACT.Ln, bias=eps[:, 0:1], scale=1.0 / D).then_inc(mem_ln, 1)
            act.wait_ge(mem_ln, 1)
            nc.scalar.activation(rmem, rmem, ACT.Exp, scale=-0.5).then_inc(mem_r, 1)
            act.wait_ge(memk_done, 1)
            act.wait_ge(memv_done, 1)
            act.wait_ge(scaled, 1)
            nc.scalar.activation(vm[:, 0, :, :], vraw, ACT.Copy, scale=s_v).then_inc(hi_v, 1)
            for h in range(2):
                r = slice(64 * h, 64 * h + 64)
                for half in range(2):
                    nc.scalar.activation(kst[64 * half:64 * half + 64, :, h, 0, :], kraw[r, :, :], ACT.Copy,
                                         scale=s_k[r, :]).then_inc(hi_k, 1)

            def hi_tile(k):
                nc.scalar.activation(whl[:, 0, k, :], wraw[:, k, 0:WIDE], ACT.Copy, scale=gs[:, k:k + 1]).then_inc(hi_w, 1)

            def squares(n):
                act.wait_ge(d_x, 16 * (n + 1))
                a, b = (sq0, xb0) if isinstance(n, int) and n == 0 else (sq, xb)
                nc.scalar.activation(a, b, ACT.Square).then_inc(x_sq, 1)

            def rstd(n):
                act.wait_ge(pe_rb, n + 1)
                r = (sq0 if isinstance(n, int) and n == 0 else sq)[:, 1, :]
                nc.scalar.activation(r, bank[3][:, 0:TB], ACT.Ln, bias=eps[:, 0:1], scale=1.0 / D).then_inc(rb_ln, 1)
                act.wait_ge(rb_ln, n + 1)
                nc.scalar.activation(r, r, ACT.Exp, bias=eps[:, 1:2], scale=-0.5).then_inc(rb_ok, 1)

            def x_parts(n):
                act.wait_ge(xn_ok, n + 1)
                if not isinstance(n, int) or n:
                    act.wait_ge(pe_pv, n)
                    whole = xb
                else:
                    wait_split(act, 1)
                    act.wait_ge(low_rank, 3)
                    whole = xb0
                for h in range(2):
                    k = slice(h * KT // 2, (h + 1) * KT // 2)
                    nc.scalar.activation(xn[:, 0, k, :], whole[:, k, :], ACT.Copy).then_inc(x_hi, 1)

            squares(0)
            act.wait_ge(scaled, 2)
            for k in range(KT):
                hi_tile(k)
                if k == 1:
                    rstd(0)
                if k == 4:
                    x_parts(0)

            def mixed_hi(n):
                act.wait_ge(m_sc, n + 1)
                if isinstance(n, int) and n == NB - 1:
                    act.wait_ge(pe_out, 4 * n)
                nc.scalar.activation(mhl[:, 0, :, :], mixed, ACT.Copy, scale=s_m).then_inc(m_hi, 1)

            def norm_y(j, t):
                act.wait_ge(y_add, 4 * (j + 1) + 2 * t + 2)
                act.wait_ge(pe_ms, 4 * (j + 1))
                nc.scalar.activation(junk, yb, ACT.Square, accum_out=ysum[:, 0:1]).then_inc(y_sq, 1)
                act.wait_ge(y_sq, 2 * j + t + 1)
                nc.scalar.activation(yr[:, 1:2], ysum[:, 0:1], ACT.Ln, bias=eps[:, 0:1],
                                     scale=1.0 / D).then_inc(y_ln, 1)
                act.wait_ge(y_ln, 2 * j + t + 1)
                nc.scalar.activation(yr[:, 0:1], yr[:, 1:2], ACT.Exp, scale=-0.5).then_inc(y_r, 1)

            def step(i, first, last):
                if first:
                    wait_split(act, KT - 1)
                act.wait_ge(pe_lr, i + 1)
                if not first:
                    act.wait_ge(mix_g, 2 * i)
                nc.scalar.activation(lrs[0:2 * RANK, :], bank[0][0:2 * RANK, 0:TB], ACT.Copy,
                                     scale=sc_in[0:2 * RANK, :]).then_inc(lr_out, 1)
                act.wait_ge(z_ok, 2 * (i + 1))
                nc.scalar.activation(ta, tm, ACT.Abs).then_inc(abs_ok, 1)
                act.wait_ge(abs_ok, i + 1)
                nc.scalar.activation(ta, ta, ACT.Exp, scale=-1.0).then_inc(expabs, 1)
                act.wait_ge(expabs, i + 1)
                nc.scalar.activation(ta, ta, ACT.Ln, bias=1.0).then_inc(softplus, 1)
                act.wait_ge(b_ok, 2 * (i + 1))
                nc.scalar.activation(te, tb, ACT.Exp, scale=1.0 / NORMALIZER).then_inc(eb_ok, 1)
                nc.scalar.activation(ta, tb, ACT.Exp, scale=-1.0 / NORMALIZER).then_inc(enb_ok, 1)
                act.wait_ge(bl_ok, i + 1)
                nc.scalar.activation(tm, tm, ACT.Exp, scale=1.0 / NORMALIZER).then_inc(ebl_ok, 1)
                for t in range(NT):
                    act.wait_ge(pe_v, 2 * i + t + 1)
                    nc.scalar.activation(v[:, t, :], bank[t][:, :], ACT.Copy, scale=sc_in).then_inc(v_out, 1)
                    if t == 0 and not first:
                        mixed_hi(i - 1)
                if first:
                    act.wait_ge(scaled, 3)
                    for k in range(KT):
                        nc.scalar.activation(wo[:, 0, k, :], woraw[:, k, :], ACT.Copy,
                                             scale=g_out[:, k:k + 1]).then_inc(hi_o, 1)
                    act.wait_ge(lo_o, KT)
                    act.wait_ge(hi_o, KT)

                def silu(n, b, g):
                    act.wait_ge(pe_p2, 6 * i + n)
                    nc.scalar.activation(gate[:, g:g + 2, :], bank[b][:, :].rearrange("p (a t) -> p a t", a=2),
                                         ACT.Silu, scale=sc_in).then_inc(p2_out, 1)

                silu(1, 2, 0)
                silu(2, 3, 2)
                act.wait_ge(pe_p2, 6 * i + 3)
                act.wait_ge(halo_ok, i + 1)
                nc.scalar.activation(ub[:, :, HALO:], bank[0][:, :].rearrange("p (a t) -> p a t", a=2), ACT.Copy,
                                     scale=sc_in).then_inc(p2_out, 1)
                silu(4, 1, 4)
                silu(5, 2, 6)
                nc.scalar.preload_act_table_set(EXP_LN)
                act.wait_ge(pe_p2, 6 * i + 6)
                if not first:
                    act.wait_ge(y_sq, 2 * (i - 1))
                for h in range(2):
                    r = slice(64 * h, 64 * h + 64)
                    nc.scalar.activation(qst[r, :, h, :], bank[3][r, :].rearrange("p (a t) -> p a t", a=2), ACT.Copy,
                                         scale=2.0 ** -QBITS).then_inc(qm_hi, 1)
                if not last:
                    if not first:
                        act.wait_ge(m_lo, i)
                    squares(i + 1)
                act.wait_ge(pe_ket, i + 1)
                if first:
                    act.wait_ge(cleared, 3)
                for odd in range(2):
                    r = slice(64 * odd, 64 * odd + 64)
                    nc.scalar.activation(kab[r, :, odd, :], bank[4][r, :].rearrange("p (a b) -> p a b", b=64),
                                         ACT.Copy).then_inc(ket_out, 1)

                def p_exp_of(n):
                    act.wait_ge(nmax_ok, 4 * i + n + 1)
                    if n >= 2:
                        act.wait_ge(p_lo, 4 * i + n - 1)
                    else:
                        act.wait_ge(pooled, 4 * (i + 1))
                        if not first:
                            act.wait_ge(pe_pt, 4 * i)
                    for h in range(2):
                        a = nc.scalar.activation(pr[n % 2][:, h, :], bank[2 + n % 2][:, h * 256:(h + 1) * 256], ACT.Exp,
                                                 bias=nm[:, 2 * n + h:2 * n + h + 1], scale=sc_ms,
                                                 accum_out=psum_p[:, 2 * n + h:2 * n + h + 1])
                    a.then_inc(p_exp, 1)

                def p_hi_of(n):
                    act.wait_ge(pn_ok, 4 * i + n + 1)
                    if n >= 2:
                        act.wait_ge(pe_pt, 4 * i + n - 1)
                    nc.scalar.activation(phl[n % 2][:, 0, :, :], pr[n % 2], ACT.Copy).then_inc(p_hi, 1)

                p_exp_of(0)
                p_exp_of(1)
                p_hi_of(0)
                p_hi_of(1)
                p_exp_of(2)
                p_exp_of(3)
                p_hi_of(2)
                if not first:
                    norm_y(i - 1, 0)
                p_hi_of(3)
                if not last:
                    rstd(i + 1)

                for p, b in ((0, 5), (1, 4)):
                    act.wait_ge(pe_o, 2 * i + p + 1)
                    nc.scalar.activation(osq[p], bank[b][:, :].rearrange("p (a t) -> p a t", a=2),
                                         ACT.Square).then_inc(o_sq, 1)
                if not last:
                    x_parts(i + 1)
                for p in range(NPAIR):
                    act.wait_ge(pe_msq, 2 * i + p + 1)
                    nc.scalar.activation(osq[p], bank[6 + p][:, :].rearrange("p (a t) -> p a t", a=2), ACT.Ln,
                                         bias=eps[:, 0:1], scale=1.0 / DV).then_inc(o_ln, 1)
                    act.wait_ge(o_ln, 2 * i + p + 1)
                    nc.scalar.activation(osq[p], osq[p], ACT.Exp, scale=-0.5).then_inc(o_r, 1)
                if not first:
                    norm_y(i - 1, 1)

            def tail(n):
                mixed_hi(n - 1)
                norm_y(n - 1, 0)
                norm_y(n - 1, 1)

            run_blocks(act, step, tail)

        @block.vector
        def _(dve):
            nc.vector.memset(pwb, 0.0).then_inc(cleared, 1)
            nc.vector.memset(keep[:, :], 1.0).then_inc(gk_ok, 1)
            dve.wait_ge(gk_ok, 1)
            nc.vector.memset(keep[:, 0:TB:CHUNK], 0.0).then_inc(gk_ok, 1)

            steps = [0]

            def after(ins):
                steps[0] += 1
                ins.then_inc(max_in, 1)
                dve.wait_ge(max_in, steps[0])

            def exponents(src, s, inv, m_tmp=m_tmp, e_tmp=e_tmp):
                after(nc.vector.tensor_scalar(m_tmp, src, TINY, None, ALU.max))
                after(nc.vector.tensor_scalar(e_tmp.bitcast(I32), m_tmp.bitcast(I32), EXP_MASK, None, ALU.bitwise_and))
                nc.vector.tensor_scalar(s.bitcast(I32), e_tmp.bitcast(I32), -1.0, SCALE_FIELD, ALU.mult, ALU.add)
                after(nc.vector.tensor_scalar(inv.bitcast(I32), e_tmp.bitcast(I32), INV_FIELD, None, ALU.add))

            def normalise(n):
                dve.wait_ge(rb_ok, n + 1)
                r = sq[:, 1:2, :].broadcast_to([P, KT, TB])
                nc.vector.tensor_tensor(xb, xb, r, ALU.mult).then_inc(xn_ok, 1)

            dve.wait_ge(d_vec, 16 * 5)
            dve.wait_ge(fold_out, 4)
            for k in range(KT):
                if k == 0:
                    dve.wait_ge(mem_r, 1)
                    for m in range(KT):
                        nc.vector.scalar_tensor_tensor(memb[:, m, :], memb[:, m, :], g_mem[:, m:m + 1], rmem,
                                                       ALU.mult, ALU.mult).then_inc(mem_n, 1)
                dve.wait_ge(d_w[k], 32)
                a = nc.vector.tensor_reduce(wmx[:, 0, k:k + 1], wraw[:, k, :], AX.X, ALU.max, apply_absolute_value=True)
                if k == MEM_AFTER:
                    dve.wait_ge(memk_done, 1)
                    dve.wait_ge(memv_done, 1)
                    nc.vector.tensor_reduce(kvmax[:, 0:1], vraw, AX.XY, ALU.max, apply_absolute_value=True)
                    nc.vector.tensor_reduce(kvmax[:, 1:2], kraw, AX.XY, ALU.max,
                                            apply_absolute_value=True).then_inc(mmax_ok, 1)
                if k == MEM_AFTER + 1:
                    dve.wait_ge(max_all, 1)
                    exponents(kvmax[:, 2:4], s_vk, i_vk, m_vk, e_vk)
                    nc.vector.tensor_scalar(kvmax[:, 2:4], s_vk, 1.0, None, ALU.mult).then_inc(scaled, 1)
            after(a)
            after(nc.vector.tensor_tensor(wmx[:, 0, :], wmx[:, 0, :], g_in, ALU.mult))
            nc.vector.tensor_reduce(mmax[:, 1:2], wmx[:, 0, :], AX.X, ALU.max,
                                    apply_absolute_value=True).then_inc(mmax_ok, 1)
            dve.wait_ge(max_all, 2)
            exponents(mmax[:, 2:3], s_w, i_w)
            nc.vector.tensor_scalar(sc_q, i_w, 2.0 ** -XBITS * QSCALE, None, ALU.mult)
            nc.vector.tensor_scalar(sc_in, i_w, 2.0 ** -XBITS, None, ALU.mult)
            nc.vector.tensor_scalar(sc_ms, i_w, i_k, 2.0 ** (QBITS - XBITS) * MSCALE, ALU.mult, ALU.mult)
            nc.vector.tensor_scalar(sc_neg, i_w, i_k, -2.0 ** (QBITS - XBITS) * MSCALE, ALU.mult, ALU.mult)
            nc.vector.tensor_scalar(gs, g_in, s_w, None, ALU.mult).then_inc(scaled, 1)
            dve.wait_ge(scaled, 1)
            dve.wait_ge(hi_v, 1)
            nc.vector.scalar_tensor_tensor(vm[:, 1, :, :], vraw, s_v, vm[:, 0, :, :], ALU.mult,
                                           ALU.subtract).then_inc(lo_v, 1)
            dve.wait_ge(hi_k, 4)
            for h in range(2):
                r = slice(64 * h, 64 * h + 64)
                for half in range(2):
                    nc.vector.scalar_tensor_tensor(kst[64 * half:64 * half + 64, :, h, 1, :], kraw[r, :, :], s_k[r, :],
                                                   kst[r, :, h, 0, :], ALU.mult, ALU.subtract).then_inc(lo_k, 1)
            dve.wait_ge(scaled, 2)
            for k in range(KT):
                dve.wait_ge(hi_w, k + 1)
                nc.vector.scalar_tensor_tensor(whl[:, 1, k, :], wraw[:, k, 0:WIDE], gs[:, k:k + 1],
                                               whl[:, 0, k, :], ALU.mult, ALU.subtract).then_inc(lo_w, 1)

            def mixed_lo(n):
                dve.wait_ge(m_all, n + 1)
                nc.vector.tensor_scalar(m_tmp, mmax[:, 2:3], TINY, None, ALU.max).then_inc(m_tiny, 1)
                dve.wait_ge(m_tiny, n + 1)
                nc.vector.tensor_scalar(e_tmp.bitcast(I32), m_tmp.bitcast(I32), EXP_MASK, None,
                                        ALU.bitwise_and).then_inc(m_exp, 1)
                dve.wait_ge(m_exp, n + 1)
                nc.vector.tensor_scalar(i_m.bitcast(I32), e_tmp.bitcast(I32), INV_FIELD, None,
                                        ALU.add).then_inc(m_inv, 1)
                nc.vector.tensor_scalar(s_m.bitcast(I32), e_tmp.bitcast(I32), -1.0, SCALE_FIELD, ALU.mult,
                                        ALU.add).then_inc(m_sc, 1)
                dve.wait_ge(m_inv, n + 1)
                nc.vector.tensor_scalar(sc_out, i_m, i_o, None, ALU.mult).then_inc(sc_ok, 1)
                if isinstance(n, int) and n == NB - 1:
                    norm_rows(n - 1, 1)
                dve.wait_ge(m_hi, n + 1)
                nc.vector.scalar_tensor_tensor(mhl[:, 1, :, :], mixed, s_m, mhl[:, 0, :, :], ALU.mult,
                                               ALU.subtract).then_inc(m_lo, 1)

            def add_rows(j, n):
                t, h = n // 2, n % 2
                if h == 0:
                    dve.wait_ge(d_res, 16 * (NT * j + t + 1))
                dve.wait_ge(sc_ok, j + 1)
                dve.wait_ge(pe_out, 4 * j + n + 1)
                c = slice(h * 512, (h + 1) * 512)
                nc.vector.scalar_tensor_tensor(yb[:, c], bank[h][:, :], sc_out, yb[:, c], ALU.mult,
                                               ALU.add).then_inc(y_add, 1)

            def norm_rows(j, t):
                dve.wait_ge(y_add, 4 * (j + 1) + 2 * t + 2)
                dve.wait_ge(y_r, NT * j + t + 1)
                nc.vector.scalar_tensor_tensor(yb, yb, yr[:, 0:1], fg[:, :], ALU.mult, ALU.mult).then_inc(y_ok, 1)

            for n in range(4):
                nc.vector.memset(nm[:, n:n + 1], 0.0).then_inc(y_add, 1)

            def step(i, first, last):
                dve.wait_ge(pe_logit, i + 1)
                if not first:
                    dve.wait_ge(p_lo, 4 * i)
                    dve.wait_ge(pe_pt, 4 * i)
                for j in range(2):
                    nc.vector.tensor_scalar(tm[:, j, :], bank[3][:, j * TB:(j + 1) * TB], b_gk[:, j:j + 1], None,
                                            ALU.add).then_inc(z_ok, 1)
                dve.wait_ge(z_ok, 2 * (i + 1))
                dve.wait_ge(softplus, i + 1)
                nc.vector.scalar_tensor_tensor(tm, tm, 0.0, ta, ALU.min, ALU.subtract).then_inc(gk_ok, 1)
                dve.wait_ge(gk_ok, i + 3)
                for j in range(2):
                    nc.vector.tensor_tensor_scan(tb[:, j, :], keep[:, :], tm[:, j, :], 0.0, ALU.mult,
                                                 ALU.add).then_inc(b_ok, 1)
                dve.wait_ge(b_ok, 2 * (i + 1))
                b4 = tb.rearrange("p a (c t) -> p (a c) t", t=CHUNK)
                nc.vector.tensor_tensor(tm.rearrange("p a (c t) -> p (a c) t", t=CHUNK),
                                        b4[:, :, CHUNK - 1:CHUNK].broadcast_to([P, 2 * NC, CHUNK]), b4,
                                        ALU.subtract).then_inc(bl_ok, 1)
                dve.wait_ge(eb_ok, i + 1)
                dve.wait_ge(pe_q, i + 1)
                if first:
                    dve.wait_ge(cleared, 2)
                else:
                    dve.wait_ge(pe_o, 2 * i)
                for h in range(2):
                    r = slice(64 * h, 64 * h + 64)
                    nc.vector.scalar_tensor_tensor(qb[r, :, h, :], bank[1][r, :].rearrange("p (a t) -> p a t", a=2),
                                                   sc_q[r, :], te[r, :, :], ALU.mult, ALU.mult).then_inc(q_ok, 1)
                nc.vector.tensor_copy(dec[:, :, :], te[:, :, CHUNK - 1:TB:CHUNK]).then_inc(dec_ok, 1)
                dve.wait_ge(enb_ok, i + 1)
                dve.wait_ge(pe_k, i + 1)
                if not first:
                    dve.wait_ge(pe_msq, 2 * i)
                k3 = bank[2][:, :].rearrange("p (a t) -> p a t", a=2)
                nc.vector.scalar_tensor_tensor(kd, k3, sc_in, ta, ALU.mult, ALU.mult).then_inc(kd_ok, 1)
                dve.wait_ge(ebl_ok, i + 1)
                nc.vector.scalar_tensor_tensor(ke, k3, sc_in, tm, ALU.mult, ALU.mult).then_inc(ke_ok, 1)
                if first:
                    dve.wait_ge(d_wout, 16)
                    for k in range(KT):
                        a = nc.vector.tensor_reduce(wmx[:, 1, k:k + 1], woraw[:, k, :], AX.X, ALU.max, apply_absolute_value=True)
                    after(a)
                    after(nc.vector.tensor_tensor(wmx[:, 1, :], wmx[:, 1, :], g_out, ALU.mult))
                    nc.vector.tensor_reduce(mmax[:, 1:2], wmx[:, 1, :], AX.X, ALU.max,
                                            apply_absolute_value=True).then_inc(mmax_ok, 1)
                    dve.wait_ge(max_all, 3)
                    exponents(mmax[:, 2:3], s_o, i_o)
                    after(nc.vector.tensor_scalar(g_out, g_out, s_o, None, ALU.mult))
                    nc.vector.tensor_copy(mmax[:, 3:4], mmax[:, 2:3]).then_inc(scaled, 1)
                    for k in range(KT):
                        dve.wait_ge(hi_o, k + 1)
                        nc.vector.scalar_tensor_tensor(wo[:, 1, k, :], woraw[:, k, :], g_out[:, k:k + 1],
                                                       wo[:, 0, k, :], ALU.mult, ALU.subtract).then_inc(lo_o, 1)
                if not first:
                    mixed_lo(i - 1)
                for w, (r, a, s) in enumerate(((0, 0, s2), (64, 0, s4), (0, 1, s2), (64, 1, s4))):
                    dve.wait_ge(w_sum, 4 * (i + 1))
                    dve.wait_ge(halo_ok, i + 2)
                    rr = slice(r, r + 64)
                    inv = 1.0 / (2, 4, 8, 16)[w]
                    if not first:
                        nc.vector.scalar_tensor_tensor(ub[rr, a, HALO:], s[rr, a, HALO:], inv, ub[rr, a, HALO:],
                                                       ALU.mult, ALU.subtract).then_inc(pooled, 1)
                    else:
                        nc.vector.tensor_tensor(s[rr, a, HALO:2 * HALO], s[rr, a, HALO:2 * HALO], cnt[rr, a, :],
                                                ALU.mult).then_inc(cut, 1)
                        nc.vector.scalar_tensor_tensor(ub[rr, a, 2 * HALO:], s[rr, a, 2 * HALO:], inv,
                                                       ub[rr, a, 2 * HALO:], ALU.mult, ALU.subtract)
                        dve.wait_ge(cut, w + 1)
                        nc.vector.tensor_tensor(ub[rr, a, HALO:2 * HALO], s[rr, a, HALO:2 * HALO],
                                                ub[rr, a, HALO:2 * HALO], ALU.subtract).then_inc(pooled, 1)
                for h in range(2):
                    r, other = slice(64 * h, 64 * h + 64), slice(64 - 64 * h, 128 - 64 * h)
                    dve.wait_ge(qm_hi, 2 * i + h + 1)
                    nc.vector.scalar_tensor_tensor(qst[other, :, h, :], bank[3][r, :].rearrange("p (a t) -> p a t", a=2),
                                                   2.0 ** -QBITS, qst[r, :, h, :], ALU.mult,
                                                   ALU.subtract).then_inc(qm_lo, 1)
                mask = causal[:, :].bitcast(I32).unsqueeze(1).broadcast_to([P, 4, P])

                def masked(t):
                    if first:
                        dve.wait_ge(built, 3)
                        dve.wait_ge(cleared, 4)
                    dve.wait_ge(pe_sc, 2 * i + t + 1)
                    nc.vector.memset(idle[:, t:t + 1], 0.0)
                    nc.vector.copy_predicated(sT[:, t, :, :], mask, bank[6 + t][:, :].rearrange("p (a b) -> p a b", b=P)
                                              ).then_inc(sT_ok, 1)

                def mem_max(n):
                    dve.wait_ge(pe_ms, 4 * i + n + 1)
                    nc.vector.tensor_reduce(mx[:, 2 * n:2 * n + 2], bank[2 + n % 2][:, :].rearrange("p (h m) -> p h m", h=2),
                                            AX.X, ALU.max).then_inc(max_ok, 1)
                    dve.wait_ge(max_ok, 4 * i + n + 1)
                    nc.vector.tensor_scalar(nm[:, 2 * n:2 * n + 2], mx[:, 2 * n:2 * n + 2], sc_neg, None,
                                            ALU.mult).then_inc(nmax_ok, 1)

                def p_norm(n):
                    dve.wait_ge(p_exp, 4 * i + n + 1)
                    nc.vector.reciprocal(rsum[:, 2 * n:2 * n + 2], psum_p[:, 2 * n:2 * n + 2]).then_inc(rs_ok, 1)
                    dve.wait_ge(rs_ok, 4 * i + n + 1)
                    r = rsum[:, 2 * n:2 * n + 2].unsqueeze(2).broadcast_to([P, 2, NMEM])
                    nc.vector.tensor_tensor(pr[n % 2], pr[n % 2], r, ALU.mult).then_inc(pn_ok, 1)

                def state(c):
                    t, odd = c // 2, c % 2
                    dve.wait_ge(pe_st, 2 * i + t + 1)
                    if c == 0:
                        dve.wait_ge(s_carry, i + 1)
                        dve.wait_ge(dec_ok, i + 1)
                    else:
                        dve.wait_ge(s_ok, 4 * i + c)
                    for h in range(HEADS):
                        p, r = h // 2, slice(64 * (h % 2), 64 * (h % 2) + 64)
                        a = nc.vector.scalar_tensor_tensor(
                            S[r, c + 1, p, :], S[r, c, p, :], dec[r, p, c:c + 1],
                            bank[5 - t][64 * odd:64 * odd + 64, h * DV:(h + 1) * DV], ALU.mult, ALU.add)
                    a.then_inc(s_ok, 1)

                def pt_copy(n, b):
                    t, p = n // NPAIR, n % NPAIR
                    dve.wait_ge(pe_pt, 4 * i + n + 1)
                    dve.wait_ge(pe_p2, 6 * (i + 1))
                    nc.vector.tensor_copy(pt[:, p, :, t * P:(t + 1) * P],
                                          b16[b].rearrange("p (a b) -> p a b", b=P)).then_inc(pt_out, 1)

                def head(p, b):
                    dve.wait_ge(o_r, 2 * i + p + 1)
                    nc.vector.tensor_tensor(osq[p], osq[p], gate[:, 2 * p:2 * p + 2, :], ALU.mult).then_inc(og_ok, 1)
                    dve.wait_ge(og_ok, 2 * i + p + 1)
                    nc.vector.tensor_tensor(mixed[:, 2 * p:2 * p + 2, :], bank[b][:, :].rearrange("p (a t) -> p a t", a=2),
                                            osq[p], ALU.mult).then_inc(mix_g, 1)

                def rows(n):
                    if not first:
                        add_rows(i - 1, n)

                masked(0)
                masked(1)
                mem_max(0)
                mem_max(1)
                p_norm(0)
                p_norm(1)
                rows(0)
                state(0)
                state(1)
                mem_max(2)
                mem_max(3)
                pt_copy(0, 6)
                p_norm(2)
                p_norm(3)
                rows(1)
                state(2)
                pt_copy(1, 7)
                state(3)
                pt_copy(2, 6)
                if not first:
                    norm_rows(i - 1, 0)
                pt_copy(3, 7)
                if not last:
                    normalise(i + 1)
                    dve.wait_ge(xn_ok, i + 2)
                rows(2)
                dve.wait_ge(p2_out, 5 * i + 5)
                dve.wait_ge(pooled, 4 * (i + 1))
                nc.vector.tensor_tensor(mixed[:, 4:6, :], ub[:, :, HALO:], gate[:, 4:6, :], ALU.mult).then_inc(mix_p, 1)
                dve.wait_ge(pe_pv, i + 1)
                nc.vector.scalar_tensor_tensor(mixed[:, 6:8, :], bank[2][:, :].rearrange("p (a t) -> p a t", a=2), i_v,
                                               gate[:, 6:8, :], ALU.mult, ALU.mult).then_inc(mix_m, 1)
                if not last:
                    rows(3)
                head(0, 5)
                head(1, 4)
                dve.wait_ge(mix_p, i + 1)
                dve.wait_ge(mix_m, i + 1)
                dve.wait_ge(mix_g, 2 * (i + 1))
                nc.vector.tensor_reduce(mmax[:, 1:2], mixed, AX.XY, ALU.max,
                                        apply_absolute_value=True).then_inc(mmax_ok, 1)
                if last:
                    rows(3)
                elif not first:
                    norm_rows(i - 1, 1)

            def tail(n):
                mixed_lo(n - 1)
                for t in range(NT):
                    add_rows(n - 1, 2 * t)
                    add_rows(n - 1, 2 * t + 1)
                    norm_rows(n - 1, t)

            m_tiny, m_exp, m_inv, sc_ok, cut = (sem(n) for n in ("m_tiny", "m_exp", "m_inv", "sc_ok", "cut"))
            run_blocks(dve, step, tail)

        @block.gpsimd
        def _(pool):
            nc.gpsimd.memset(ones[:, :], 1.0).then_inc(built, 1)
            nc.gpsimd.memset(eps[:, 0:1], EPS)
            nc.gpsimd.memset(eps[:, 1:2], float(np.log(2.0 ** XBITS)))
            nc.gpsimd.memset(ident[:, :], 0.0).then_inc(ident_ok, 1)
            nc.gpsimd.memset(causal[:, :], 1.0).then_inc(ident_ok, 1)
            pool.wait_ge(ident_ok, 2)
            nc.gpsimd.affine_select(out=ident[:, :], in_=ident[:, :], compare_op=ALU.not_equal, fill=1.0, base=0,
                                    pattern=[[-1, P]], channel_multiplier=1).then_inc(ident_ok, 1)
            nc.gpsimd.affine_select(out=causal[:, :], in_=causal[:, :], compare_op=ALU.is_ge, fill=0.0, base=0,
                                    pattern=[[1, P]], channel_multiplier=-1).then_inc(ident_ok, 1)
            pool.wait_ge(ident_ok, 4)
            nc.gpsimd.memset(causal[0:64, 64:128], 0.0).then_inc(built, 1)
            nc.gpsimd.tensor_copy(ident16[:, :], ident[:, :]).then_inc(built, 1)

            def fold_rows(buf, n0, signal):
                for n, half in enumerate((4, 2, 1)):
                    if n:
                        pool.wait_ge(signal, n0 + n)
                    nc.gpsimd.tensor_tensor(buf[:, 0:half, :], buf[:, 0:half, :], buf[:, half:2 * half, :],
                                            ALU.add).then_inc(signal, 1)

            def x_lo_of(n):
                whole = xb0 if isinstance(n, int) and n == 0 else xb
                for h in range(2):
                    k = slice(h * KT // 2, (h + 1) * KT // 2)
                    pool.wait_ge(x_hi, 2 * n + h + 1)
                    nc.gpsimd.tensor_tensor(xn[:, 1, k, :], whole[:, k, :], xn[:, 0, k, :],
                                            ALU.subtract).then_inc(x_lo, 1)

            pool.wait_ge(mem_sq, 1)
            fold_rows(msq, 0, mem_sum)
            pool.wait_ge(mmax_ok, 1)
            nc.gpsimd.partition_all_reduce(kvmax[:, 2:4], kvmax[:, 0:2], P, RMAX).then_inc(max_all, 1)
            pool.wait_ge(mmax_ok, 2)
            nc.gpsimd.partition_all_reduce(mmax[:, 2:3], mmax[:, 1:2], P, RMAX).then_inc(max_all, 1)
            pool.wait_ge(x_sq, 1)
            fold_rows(sq0, 0, sq_add)
            pool.wait_ge(scaled, 2)
            lr = wraw[:, :, CLR:DIN]
            nc.gpsimd.tensor_tensor(lr, lr, gs.unsqueeze(2).broadcast_to([P, KT, RANK]), ALU.mult).then_inc(low_rank, 1)
            pool.wait_ge(low_rank, 1)
            nc.gpsimd.tensor_copy(wlr[:, :, 0:RANK], lr).then_inc(low_rank, 1)
            pool.wait_ge(low_rank, 2)
            nc.gpsimd.tensor_tensor(wlr[:, :, RANK:], lr, wlr[:, :, 0:RANK], ALU.subtract).then_inc(low_rank, 1)
            pool.wait_ge(rb_ok, 1)
            nc.gpsimd.tensor_tensor(xb0, xb0, sq0[:, 1:2, :].broadcast_to([P, KT, TB]), ALU.mult).then_inc(xn_ok, 1)
            x_lo_of(0)
            wait_split(pool, KT - 1)
            nc.gpsimd.memset(ub[:, :, 0:HALO], 0.0).then_inc(halo_ok, 1)
            nc.gpsimd.memset(qb, 0.0).then_inc(cleared, 1)
            pool.wait_ge(mmax_ok, 3)
            nc.gpsimd.partition_all_reduce(mmax[:, 2:3], mmax[:, 1:2], P, RMAX).then_inc(max_all, 1)
            pool.wait_ge(hi_o, KT)
            pool.wait_ge(lo_o, KT)
            nc.gpsimd.memset(kab, 0.0).then_inc(cleared, 1)
            nc.gpsimd.memset(sT, 0.0).then_inc(cleared, 1)
            nc.gpsimd.memset(S[:, 0, :, :], 0.0).then_inc(s_carry, 1)

            def p_lo_of(i, n):
                pool.wait_ge(p_hi, 4 * i + n + 1)
                nc.gpsimd.tensor_tensor(phl[n % 2][:, 1, :, :], pr[n % 2], phl[n % 2][:, 0, :, :],
                                        ALU.subtract).then_inc(p_lo, 1)

            def step(i, first, last):
                L = HALO + TB
                pool.wait_ge(p2_out, 5 * i + 3)
                pool.wait_ge(ke_ok, i + 1)
                pool.wait_ge(q_ok, 2 * (i + 1))
                nc.gpsimd.tensor_tensor(s2[:, :, 1:L], ub[:, :, 1:L], ub[:, :, 0:L - 1], ALU.add).then_inc(w_sum, 1)
                pool.wait_ge(w_sum, 4 * i + 1)
                nc.gpsimd.tensor_tensor(s4[:, :, 3:L], s2[:, :, 3:L], s2[:, :, 1:L - 2], ALU.add).then_inc(w_sum, 1)
                nc.gpsimd.tensor_copy(ub[:, :, 0:HALO], ub[:, :, TB:TB + HALO]).then_inc(halo_ok, 1)
                pool.wait_ge(w_sum, 4 * i + 2)
                nc.gpsimd.tensor_tensor(s2[:, 1, 7:L], s4[:, 1, 7:L], s4[:, 1, 3:L - 4], ALU.add).then_inc(w_sum, 1)
                pool.wait_ge(w_sum, 4 * i + 3)
                nc.gpsimd.tensor_tensor(s4[:, 1, 15:L], s2[:, 1, 15:L], s2[:, 1, 7:L - 8], ALU.add).then_inc(w_sum, 1)
                if not last:
                    pool.wait_ge(x_sq, i + 2)
                    fold_rows(sq, 3 * (i + 1), sq_add)
                for n in range(4):
                    p_lo_of(i, n)
                if not last:
                    x_lo_of(i + 1)
                if not first:
                    pool.wait_ge(m_sc, i)
                pool.wait_ge(mmax_ok, i + 4)
                nc.gpsimd.tensor_tensor(idle[:, 2:3], eps[:, 0:1], eps[:, 1:2], ALU.add)
                if not last:
                    nc.gpsimd.tensor_copy(S[:, 0, :, :], S[:, NC, :, :]).then_inc(s_carry, 1)
                nc.gpsimd.partition_all_reduce(mmax[:, 2:3], mmax[:, 1:2], P, RMAX).then_inc(m_all, 1)

            run_blocks(pool, step, lambda n: None)


def kernel(**inputs):
    import concourse.bacc as bacc
    from concourse.bass_utils import run_bass_kernel_spmd

    a = {k: np.asarray(v) for k, v in inputs.items()}
    T = a["x"].shape[1]

    def tiled(w):
        return np.ascontiguousarray(w.reshape(-1, P, w.shape[1]).transpose(1, 0, 2))

    def column(g):
        return g.reshape(-1, P).T

    w = a["w_in"]
    sizes = (256, 256, 512, RANK, 512, 256, 256, 256, 256)
    q, k, v, lr, gg, u, gp, qm, gm = np.split(w, np.cumsum(sizes)[:-1], axis=1)
    counts = np.zeros((P, 2, HALO), np.float32)
    for g, win in enumerate((2, 4, 8, 16)):
        counts[64 * (g % 2):64 * (g % 2) + 64, g // 2] = 1.0 / np.minimum(np.arange(HALO) + 1, win)
    unit = np.ones((P, 2), np.float32)
    arrays = {
        "xt": np.ascontiguousarray(a["x"][0].T.reshape(KT, P, T // TB, TB).transpose(2, 1, 0, 3)),
        "x": np.ascontiguousarray(a["x"][0]),
        "memt": tiled(np.ascontiguousarray(a["mem"][0].T)),
        "w_in": tiled(np.concatenate([q, k, v, gg, gp, gm, qm, lr], axis=1)),
        "w_ut": tiled(np.ascontiguousarray(u.T)),
        "w_gk_up": np.ascontiguousarray(a["w_gk_up"]),
        "vecs": np.ascontiguousarray(np.concatenate(
            [column(a["norm_g"]), column(a["mem_norm_g"]), column(a["b_gk"])]
            + [column(a["gla_norm_g"])] * HEADS + [column(a["pool_scale"]), unit], axis=1)),
        "pool_w": np.ascontiguousarray(a["pool_w"]),
        "counts": counts,
        "w_mem": tiled(a["w_mem_kv"]),
        "w_out": tiled(a["w_out"]),
        "final_g": np.ascontiguousarray(a["final_g"]),
    }
    nc = bacc.Bacc("TRN2", target_bir_lowering=False, num_devices=1)
    args = [nc.dram_tensor(f"in_{n}", x.shape, mybir.dt.from_np(x.dtype), kind="ExternalInput").ap()
            for n, x in arrays.items()]
    out = nc.dram_tensor("out", (T, D), F32, kind="ExternalOutput").ap()
    hybrid_block(nc, *args, out)
    r = run_bass_kernel_spmd(nc, [{f"in_{n}": x for n, x in arrays.items()}], core_ids=[0])
    return r.results[0]["out"].reshape(a["x"].shape)
```
